# Optimizing a Trainium2 kernel written in Bass

```python
import jax, jax.numpy as jnp
from jax import lax
import numpy as np

D_MODEL = 1024
BATCH = 1
SEQ = 2048
DEPTH = 1

GRID_W = 64
CTX_LEN = 256
N_HEADS_NA = 8
HEAD_DIM = 64
D_NA = N_HEADS_NA * HEAD_DIM
NA_KH = 8
NA_KW = 16
D_SG = D_MODEL - D_NA
N_GROUPS_SG = 8
SG_GROUP_DIM = D_SG // N_GROUPS_SG
CHUNK = 128
D_MIX = D_NA + D_SG
D_IN = 3 * D_NA + 2 * D_SG
N_EXPERTS = 16
EC_CAPACITY_FACTOR = 2
D_EXPERT = 1536
N_MOD = 6
EPS = 1e-6
NEG_INF = -1e30

kernel_name = "hybrid_na_gmlp_ec_moe_dit"

def rmsnorm(x, g):
    xf = x.astype(jnp.float32)
    xf = xf * lax.rsqrt(jnp.mean(xf * xf, axis=-1, keepdims=True) + EPS)
    return xf.astype(x.dtype) * g

def layernorm(x, g):
    xf = x.astype(jnp.float32)
    mu = jnp.mean(xf, axis=-1, keepdims=True)
    var = jnp.mean(jnp.square(xf - mu), axis=-1, keepdims=True)
    return ((xf - mu) * lax.rsqrt(var + EPS)).astype(x.dtype) * g

def modulate(h, shift, scale):
    return h * (1 + scale) + shift

def split_in(z):
    q = z[..., :D_NA]
    k = z[..., D_NA:2 * D_NA]
    v = z[..., 2 * D_NA:3 * D_NA]
    u = z[..., 3 * D_NA:3 * D_NA + D_SG]
    zg = z[..., 3 * D_NA + D_SG:]
    return q, k, v, u, zg

def heads(t):
    return t.reshape(t.shape[:-1] + (N_HEADS_NA, HEAD_DIM))

def neighbourhood_attention(q, k, v, k_ctx, v_ctx, rpb):
    b, n, h, dh = q.shape
    rows = n // GRID_W
    kh = min(NA_KH, rows)
    r = np.arange(rows)
    row_start = np.clip(r - kh // 2, 0, rows - kh)
    row_idx = row_start[:, None] + np.arange(kh)[None, :]
    col = np.arange(GRID_W)
    col_start = np.clip(col - NA_KW // 2, 0, GRID_W - NA_KW)
    col_mask = (col[None, :] >= col_start[:, None]) & (col[None, :] < col_start[:, None] + NA_KW)
    row_off = row_idx - r[:, None] + NA_KH - 1
    col_off = np.clip(col[None, :] - col[:, None] + NA_KW - 1, 0, 2 * NA_KW - 2)
    bias = rpb[:, row_off[:, None, :, None], col_off[None, :, None, :]]

    qg = q.reshape(b, rows, GRID_W, h, dh)
    kg = k.reshape(b, rows, GRID_W, h, dh)[:, row_idx]
    vg = v.reshape(b, rows, GRID_W, h, dh)[:, row_idx]
    scale = dh ** -0.5
    s_nb = jnp.einsum('brqhd,brikhd->bhrqik', qg, kg).astype(jnp.float32) * scale + bias.astype(jnp.float32)[None]
    s_nb = jnp.where(col_mask[:, None, :], s_nb, NEG_INF)
    s_ctx = jnp.einsum('brqhd,bjhd->bhrqj', qg, k_ctx).astype(jnp.float32) * scale
    s = jnp.concatenate([s_nb.reshape(b, h, rows, GRID_W, kh * GRID_W), s_ctx], axis=-1)
    p = jax.nn.softmax(s, axis=-1).astype(v.dtype)
    p_nb = p[..., :kh * GRID_W].reshape(b, h, rows, GRID_W, kh, GRID_W)
    p_ctx = p[..., kh * GRID_W:]
    o = jnp.einsum('bhrqik,brikhd->brqhd', p_nb, vg) + jnp.einsum('bhrqj,bjhd->brqhd', p_ctx, v_ctx)
    return o.reshape(b, n, h * dh)

def context_attention(q, k, v):
    b, l, h, dh = q.shape
    s = jnp.einsum('bqhd,bkhd->bhqk', q, k).astype(jnp.float32) * dh ** -0.5
    p = jax.nn.softmax(s, axis=-1).astype(v.dtype)
    return jnp.einsum('bhqk,bkhd->bqhd', p, v).reshape(b, l, h * dh)

def chunk_gmlp(u, zg, w_s, b_s, g_norm):
    b, n, _ = u.shape
    u = jax.nn.gelu(u)
    zg = layernorm(jax.nn.gelu(zg), g_norm)
    zc = zg.reshape(b, n // CHUNK, CHUNK, N_GROUPS_SG, SG_GROUP_DIM)
    sp = jnp.einsum('gpq,bcqgd->bcpgd', w_s, zc) + b_s.T[None, None, :, :, None]
    return u * sp.reshape(b, n, D_SG)

def mix_out(o_a, o_b, out_norm_a, out_norm_b, w_out):
    o = jnp.concatenate([rmsnorm(o_a, out_norm_a), rmsnorm(o_b, out_norm_b)], axis=-1)
    return o @ w_out

def expert_choice_ffn(h, w_router, w_gate, w_up, w_down):
    b, n, d = h.shape
    cap = EC_CAPACITY_FACTOR * n // N_EXPERTS
    aff = jax.nn.softmax((h @ w_router).astype(jnp.float32), axis=-1)
    gates, idx = lax.top_k(jnp.swapaxes(aff, 1, 2), cap)
    xs = jax.vmap(lambda hb, ib: hb[ib])(h, idx)
    a = jnp.einsum('becd,edf->becf', xs, w_gate)
    up = jnp.einsum('becd,edf->becf', xs, w_up)
    y = jnp.einsum('becf,efd->becd', jax.nn.silu(a) * up, w_down) * gates[..., None].astype(h.dtype)
    return jax.vmap(lambda ib, yb: jnp.zeros((n, d), yb.dtype).at[ib.reshape(-1)].add(yb.reshape(-1, d)))(idx, y)

def setup_inputs(seed: int = 0) -> dict:
    key = jax.random.key(seed)
    ks = jax.random.split(key, 22)
    nrm = jax.random.normal
    f32 = jnp.float32
    return {
        "x": nrm(ks[0], (BATCH, SEQ, D_MODEL), f32),
        "c": nrm(ks[1], (BATCH, D_MODEL), f32),
        "ctx": nrm(ks[2], (BATCH, CTX_LEN, D_MODEL), f32),
        "c_ctx": nrm(ks[3], (D_MODEL,), f32),
        "w_mod": nrm(ks[4], (DEPTH, D_MODEL, N_MOD * D_MODEL), f32) * (0.5 * D_MODEL ** -0.5),
        "b_mod": nrm(ks[5], (DEPTH, N_MOD * D_MODEL), f32) * 0.01,
        "norm1": 1.0 + 0.02 * nrm(ks[6], (DEPTH, D_MODEL), f32),
        "w_in": nrm(ks[7], (DEPTH, D_MODEL, D_IN), f32) * D_MODEL ** -0.5,
        "rpb": 0.1 * nrm(ks[8], (DEPTH, N_HEADS_NA, 2 * NA_KH - 1, 2 * NA_KW - 1), f32),
        "w_s": nrm(ks[9], (DEPTH, N_GROUPS_SG, CHUNK, CHUNK), f32) * CHUNK ** -0.5,
        "b_s": 1.0 + 0.02 * nrm(ks[10], (DEPTH, N_GROUPS_SG, CHUNK), f32),
        "gmlp_norm": 1.0 + 0.02 * nrm(ks[11], (DEPTH, D_SG), f32),
        "out_norm_a": 1.0 + 0.02 * nrm(ks[12], (DEPTH, D_NA), f32),
        "out_norm_b": 1.0 + 0.02 * nrm(ks[13], (DEPTH, D_SG), f32),
        "w_out": nrm(ks[14], (DEPTH, D_MIX, D_MODEL), f32) * D_MIX ** -0.5,
        "norm2": 1.0 + 0.02 * nrm(ks[15], (DEPTH, D_MODEL), f32),
        "w_router": nrm(ks[16], (DEPTH, D_MODEL, N_EXPERTS), f32) * D_MODEL ** -0.5,
        "w_gate": nrm(ks[17], (DEPTH, N_EXPERTS, D_MODEL, D_EXPERT), f32) * D_MODEL ** -0.5,
        "w_up": nrm(ks[18], (DEPTH, N_EXPERTS, D_MODEL, D_EXPERT), f32) * D_MODEL ** -0.5,
        "w_down": nrm(ks[19], (DEPTH, N_EXPERTS, D_EXPERT, D_MODEL), f32) * D_EXPERT ** -0.5,
        "norm_final": 1.0 + 0.02 * nrm(ks[20], (D_MODEL,), f32),
    }

def reference(x, c, ctx, c_ctx, w_mod, b_mod, norm1, w_in, rpb, w_s, b_s, gmlp_norm,
              out_norm_a, out_norm_b, w_out, norm2, w_router, w_gate, w_up, w_down, norm_final):
    b = x.shape[0]
    for l in range(DEPTH):
        last = l == DEPTH - 1
        m = (jax.nn.silu(c) @ w_mod[l] + b_mod[l]).reshape(b, 1, N_MOD, D_MODEL)
        sh1, sc1, g1, sh2, sc2, g2 = (m[:, :, i] for i in range(N_MOD))
        mc = (jax.nn.silu(c_ctx) @ w_mod[l] + b_mod[l]).reshape(N_MOD, D_MODEL)
        sh1c, sc1c, g1c, sh2c, sc2c, g2c = (mc[i] for i in range(N_MOD))

        h = modulate(rmsnorm(x, norm1[l]), sh1, sc1)
        hc = modulate(rmsnorm(ctx, norm1[l]), sh1c, sc1c)
        q, k, v, u, zg = split_in(h @ w_in[l])
        if last:
            kv_c = hc @ w_in[l][:, D_NA:3 * D_NA]
            k_c, v_c = kv_c[..., :D_NA], kv_c[..., D_NA:]
        else:
            q_c, k_c, v_c, u_c, zg_c = split_in(hc @ w_in[l])
        o_a = neighbourhood_attention(heads(q), heads(k), heads(v), heads(k_c), heads(v_c), rpb[l])
        o_b = chunk_gmlp(u, zg, w_s[l], b_s[l], gmlp_norm[l])
        x_new = x + g1 * mix_out(o_a, o_b, out_norm_a[l], out_norm_b[l], w_out[l])

        if not last:
            o_ac = context_attention(heads(q_c), heads(k_c), heads(v_c))
            o_bc = chunk_gmlp(u_c, zg_c, w_s[l], b_s[l], gmlp_norm[l])
            ctx = ctx + g1c * mix_out(o_ac, o_bc, out_norm_a[l], out_norm_b[l], w_out[l])
            hc2 = modulate(rmsnorm(ctx, norm2[l]), sh2c, sc2c)
            ctx = ctx + g2c * expert_choice_ffn(hc2, w_router[l], w_gate[l], w_up[l], w_down[l])

        x = x_new
        h2 = modulate(rmsnorm(x, norm2[l]), sh2, sc2)
        x = x + g2 * expert_choice_ffn(h2, w_router[l], w_gate[l], w_up[l], w_down[l])
    return rmsnorm(x, norm_final)


_drawn_inputs = setup_inputs


def setup_inputs(seed=0):
    import zlib

    import numpy as np

    out = dict(_drawn_inputs(seed))
    spreads = {}
    factors = {'b_mod': 3.833,
     'norm1': 7.607,
     'rpb': 8.0,
     'b_s': 8.0,
     'gmlp_norm': 8.0,
     'out_norm_a': 8.0,
     'out_norm_b': 8.0,
     'norm2': 8.0,
     'norm_final': 2.964}
    for name, (base, spread) in spreads.items():
        noise = np.random.default_rng([zlib.crc32(name.encode()), seed]).standard_normal(out[name].shape)
        drawn = base * np.exp(spread * noise) if base else spread * noise
        out[name] = __import__('jax').numpy.asarray(drawn.astype(out[name].dtype))
    for name, factor in factors.items():
        out[name] = (out[name] * factor).astype(out[name].dtype)
    return out
```

```python
from contextlib import ExitStack

import concourse.bass as bass
from concourse import mybir

F32 = mybir.dt.float32
F32R = mybir.dt.float32r
BF16 = mybir.dt.bfloat16
U32 = mybir.dt.uint32
ALU = mybir.AluOpType
ACT = mybir.ActivationFunctionType
AX = mybir.AxisListType

P = 128
D = 1024
KD = D // P
SEQ = 2048
CTX = 256
TILES = SEQ // P
GRID_W = 64
ROWS = SEQ // GRID_W
HEADS = 8
DH = 64
NA = HEADS * DH
KNA = NA // P
WIN_H = 8
WIN_W = 16
RPB_H = 2 * WIN_H - 1
RPB_W = 2 * WIN_W - 1
SG = D - NA
GROUPS = 8
GD = SG // GROUPS
N_MOD = 6
EXPERTS = 16
CAP = 2 * SEQ // EXPERTS
DE = 1536
EPS = 1e-6
MASKED = -1e30
BANK = 512

SMALL = {}
for _name, _rows in (("c", KD), ("c_ctx", KD), ("norm1", KD), ("norm2", KD),
                     ("out_norm_a", KNA), ("out_norm_b", KNA), ("b_s", GROUPS)):
    SMALL[_name] = (sum(b - a for a, b in SMALL.values()), sum(b - a for a, b in SMALL.values()) + _rows)
SMALL_ROWS = max(b for _, b in SMALL.values())

KEY_ROWS = WIN_H + 1
SLOTS = RPB_H + 1
LOCAL = KEY_ROWS * GRID_W
KEYS = LOCAL + CTX
BLOCKS = ROWS // 2
EDGE = 2


def key_base(j):
    return min(max(2 * j - WIN_H // 2, 0), ROWS - KEY_ROWS)


class Chain:

    def __init__(self, eng, sem, base=0):
        self.eng, self.sem, self.base, self.n = eng, sem, base, 0

    def __call__(self, instruction):
        instruction.then_inc(self.sem, 1)
        self.n += 1
        self.eng.wait_ge(self.sem, self.base + self.n)


def apart(eng, passed):
    eng.sem_inc(passed, 1)


def each(eng, n):
    from contextlib import nullcontext
    return eng.Fori(0, n) if n > 1 else nullcontext(0)


def modulation_phase(nc, sem, io, scratch, keep):
    UNITS = N_MOD * D // BANK
    RING = 3
    w_mod = io["w_mod"][0].rearrange("(k p) (u n) -> u p k n", p=P, n=BANK)
    with ExitStack() as ctx:
        def sb(name, shape, dt=F32):
            return ctx.enter_context(nc.sbuf_tensor(f"m_{name}", shape, dt))

        small_rows = sb("small_rows", [SMALL_ROWS, P])
        cond = sb("cond", [P, 2, KD])
        wm = sb("wm", [P, RING, KD, BANK])
        bias_rows = sb("bias_rows", [2, N_MOD * D])
        mod_rows = sb("mod_rows", [2, N_MOD * D])
        mod_cols = sb("mod_cols", [P, N_MOD * KD, 2])
        rel = sb("rel", [GRID_W, HEADS * RPB_H, 2 * GRID_W])
        table = sb("table", [P, HEADS, SLOTS, GRID_W])
        ps_t = ctx.enter_context(nc.psum_tensor("ps_t", [P, BANK], F32))
        ps_m = [ctx.enter_context(nc.psum_tensor(f"ps_m{i}", [P, BANK], F32)) for i in range(2)]
        small_in = sem("small_in")
        bias_in = sem("mod_bias_in")
        wm_in = [sem(f"wm_in{i}") for i in range(RING)]
        ident_ok = sem("ident_ok")
        small_t = sem("small_t")
        small_ok = sem("small_ok")
        cond_ok = sem("cond_ok")
        mod_mm = sem("mod_mm")
        mod_row = sem("mod_row")
        mod_t = sem("mod_t")
        mod_col = sem("mod_col")
        mod_out = sem("mod_out")
        rel_zero = sem("rel_zero")
        rel_in = sem("rel_in")
        rel_out = sem("rel_out")
        table_set = sem("table_set")
        table_in = sem("table_in")
        table_cut = sem("table_cut")
        table_out = sem("table_out")
        block = ctx.enter_context(nc.Block())

        @block.sync
        def _(sp):
            for name, (a, b) in SMALL.items():
                src = {"c": io["c"], "c_ctx": io["c_ctx"].rearrange("(a d) -> a d", a=1),
                       "norm1": io["norm1"], "norm2": io["norm2"], "out_norm_a": io["out_norm_a"],
                       "out_norm_b": io["out_norm_b"], "b_s": io["b_s"][0]}[name]
                if name != "b_s":
                    src = src.rearrange("a (r p) -> (a r) p", p=P)
                sp.dma_start(small_rows[a:b, :], src).then_inc(small_in, 16)
            for u in range(UNITS):
                if u >= RING:
                    sp.wait_ge(mod_mm, u - RING + 1)
                sp.dma_start(wm[:, u % RING], w_mod[u]).then_inc(wm_in[u % RING], 16)
                if u == 3:
                    for a in range(2):
                        sp.dma_start(bias_rows[a:a + 1, :], io["b_mod"]).then_inc(bias_in, 16)
            sp.wait_ge(mod_row, UNITS)
            sp.dma_start(scratch["mod"], mod_rows[:, :]).then_inc(mod_out, 16)
            sp.wait_ge(mod_out, 16)

        @block.gpsimd
        def _(pool):
            ident = keep["ident"]
            pool.memset(ident[:, :], 0.0).then_inc(ident_ok, 1)
            pool.wait_ge(ident_ok, 1)
            pool.affine_select(out=ident[:, :], in_=ident[:, :], compare_op=ALU.not_equal, fill=1.0,
                               base=0, pattern=[[-1, P]], channel_multiplier=1).then_inc(ident_ok, 1)
            pool.memset(keep["minus_half"][:, :], -0.5)
            pool.memset(keep["eps"][:, :], EPS)
            pool.memset(rel[:, :, :], 0.0).then_inc(rel_zero, 1)
            pool.memset(table[:, :, :, :], MASKED).then_inc(table_set, 1)
            pool.wait_ge(rel_zero, 1)
            at = GRID_W - WIN_W
            rpb = io["rpb"][0].rearrange("h r c -> (h r) c").partition_broadcast(GRID_W)
            pool.dma_start(rel[:, :, at:at + RPB_W], rpb).then_inc(rel_in, 16)
            pool.wait_ge(rel_in, 16)
            pool.dma_start(scratch["rel"].rearrange("r q c -> q r c"), rel[:, :, :]).then_inc(rel_out, 16)
            pool.wait_ge(rel_out, 16)
            pool.wait_ge(table_set, 1)
            step = 2 * GRID_W - 1
            for rr in range(2):
                for h in range(HEADS):
                    skewed = bass.AP(scratch["rel"].tensor, h * RPB_H * GRID_W * 2 * GRID_W + GRID_W - 1,
                                     [[step, GRID_W], [GRID_W * 2 * GRID_W, RPB_H], [1, GRID_W]])
                    pool.dma_start(table[rr * GRID_W:(rr + 1) * GRID_W, h, rr:rr + RPB_H, :],
                                   skewed).then_inc(table_in, 16)
            pool.wait_ge(table_in, 2 * HEADS * 16)
            for rr in range(2):
                half = table[rr * GRID_W:(rr + 1) * GRID_W].rearrange("p h m k -> p (h m) k")
                low, high = half[:, :, 0:GRID_W - WIN_W], half[:, :, WIN_W:GRID_W]
                pool.affine_select(out=low, in_=low, compare_op=ALU.is_ge, fill=MASKED, base=WIN_W // 2,
                                   pattern=[[0, HEADS * SLOTS], [1, GRID_W - WIN_W]],
                                   channel_multiplier=-1).then_inc(table_cut, 1)
            pool.wait_ge(table_cut, 2)
            for rr in range(2):
                half = table[rr * GRID_W:(rr + 1) * GRID_W].rearrange("p h m k -> p (h m) k")
                low, high = half[:, :, 0:GRID_W - WIN_W], half[:, :, WIN_W:GRID_W]
                pool.affine_select(out=high, in_=high, compare_op=ALU.is_ge, fill=MASKED,
                                   base=WIN_W // 2 - 1 - WIN_W,
                                   pattern=[[0, HEADS * SLOTS], [-1, GRID_W - WIN_W]],
                                   channel_multiplier=1).then_inc(table_cut, 1)
            pool.wait_ge(table_cut, 4)
            pool.dma_start(scratch["table"], table[:, :, :, :]).then_inc(table_out, 16)
            pool.wait_ge(table_out, 16)

        @block.scalar
        def _(act):
            a, b = SMALL["c"][0], SMALL["c_ctx"][1]
            act.wait_ge(small_ok, 1)
            act.activation(cond[:, :, :].rearrange("p a k -> p (a k)"), keep["small"][:, a:b],
                           ACT.Silu).then_inc(cond_ok, 1)

        @block.tensor
        def _(pe):
            ident = keep["ident"]
            pe.wait_ge(ident_ok, 2)
            pe.wait_ge(small_in, 16 * len(SMALL))
            pe.transpose(ps_t[:, 0:SMALL_ROWS], small_rows[:, :],
                         ident[0:SMALL_ROWS, 0:SMALL_ROWS]).then_inc(small_t, 1)
            pe.wait_ge(cond_ok, 1)
            for u in range(UNITS):
                pe.wait_ge(wm_in[u % RING], 16 * (u // RING + 1))
                if u >= 2:
                    pe.wait_ge(mod_row, u - 1)
                for k in range(KD):
                    mm = pe.matmul(ps_m[u % 2][0:2, :], cond[:, :, k], wm[:, u % RING, k, :],
                                   start=(k == 0), stop=(k == KD - 1))
                mm.then_inc(mod_mm, 1)
            pe.wait_ge(mod_row, UNITS)
            for i in range(N_MOD * KD):
                t = pe.transpose(ps_t[:, 128 + 2 * i:130 + 2 * i], mod_rows[:, i * P:(i + 1) * P],
                                 ident[0:2, 0:2])
            t.then_inc(mod_t, 1)

        @block.vector
        def _(dve):
            dve.wait_ge(small_t, 1)
            dve.tensor_copy(keep["small"][:, :], ps_t[:, 0:SMALL_ROWS]).then_inc(small_ok, 1)
            dve.wait_ge(bias_in, 32)
            for u in range(UNITS):
                cols = slice(u * BANK, (u + 1) * BANK)
                dve.wait_ge(mod_mm, u + 1)
                dve.tensor_tensor(mod_rows[:, cols], ps_m[u % 2][0:2, :], bias_rows[:, cols],
                                  ALU.add).then_inc(mod_row, 1)
            dve.wait_ge(mod_t, 1)
            dve.tensor_copy(mod_cols[:, :, :].rearrange("p m a -> p (m a)"),
                            ps_t[:, 128:128 + 2 * N_MOD * KD]).then_inc(mod_col, 1)
            dve.wait_ge(mod_col, 1)
            for name, norm, part, a in (("1", "norm1", 0, 0), ("c", "norm1", 0, 1), ("2", "norm2", 3, 0)):
                lo, hi = SMALL[norm]
                scale = mod_cols[:, (part + 1) * KD:(part + 2) * KD, a]
                shift = mod_cols[:, part * KD:(part + 1) * KD, a]
                dve.scalar_tensor_tensor(out=keep["gain" + name][:, :], in0=scale, scalar=1.0,
                                         in1=keep["small"][:, lo:hi], op0=ALU.add, op1=ALU.mult)
                dve.tensor_copy(keep["shift" + name][:, :], shift)


def projection_phase(nc, sem, io, keep, tag, x_rows, n_super, tiles, blocks, gain, shift, out):
    NT = tiles * P
    NB = min(BANK, NT)
    PAIRS = tiles // 2
    HALF_K = KD // 2
    GB = 6
    w_in = io["w_in"][0].rearrange("(j k p) n -> j p k n", p=P, k=HALF_K)
    gmlp = "z" in blocks
    col_at = {"q": 0, "k": NA, "v": 2 * NA, "u": 3 * NA, "z": 3 * NA + SG}

    groups = []
    for c, name in enumerate(blocks):
        if name in "qk":
            groups += [(c, name, i, h) for h in range(NT // NB) for i in range(KNA)]
        else:
            groups += [(c, name, i, 0) for i in range(tiles)]
    first = [min(n for n, g in enumerate(groups) if g[0] == c) for c in range(len(blocks))]
    last = [max(n for n, g in enumerate(groups) if g[0] == c) for c in range(len(blocks))]
    pieces = [(pair, kh) for pair in range(PAIRS) for kh in range(2)]
    uses = []
    seen = [0] * GB
    for n in range(len(pieces)):
        banks = [2 * (n % 3), 2 * (n % 3) + 1]
        uses.append([(b, seen[b]) for b in banks])
        for b in banks:
            seen[b] += 1
    for n in range(len(groups)):
        b = n % GB
        uses.append([(b, seen[b])])
        seen[b] += 1
    NP, NG = len(pieces), len(groups)
    W_USES = [len(blocks[b::2]) for b in range(2)]
    NZ = tiles * GROUPS
    stores = [n for n, g in enumerate(groups) if g[1] in "qkvu"]
    POOL_LINKS = tiles * (3 if gmlp else 1)
    DVE_LINKS = NP + (tiles * 3 if gmlp else 0)

    with ExitStack() as ctx:
        def sb(name, shape, dt=F32):
            return ctx.enter_context(nc.sbuf_tensor(f"{tag}_{name}", shape, dt))

        hT_hi = sb("hT_hi", [P, KD, NT], F32R)
        hT_lo = sb("hT_lo", [P, KD, NT], F32R)
        w_hi = sb("w_hi", [P, 2, KD, BANK], F32R)
        w_lo = sb("w_lo", [P, 2, KD, BANK], F32R)
        w_raw = sb("w_raw", [P, 2, HALF_K, BANK])
        xin = sb("xin", [P, 2, D])
        xr = sb("xr", [P, 2, D])
        stat = sb("stat", [P, 8, 8])
        h_full = sb("h_full", [P, 2, HALF_K, 2 * P])
        stage = sb("stage", [P, 4, BANK])
        if gmlp:
            spatial = sb("spatial", [P, tiles, SG])
            act_out = sb("act_out", [P, 2, SG])
            zn = sb("zn", [P, SG])
            ws_raw = spatial[:, 0:2].rearrange("p a (g q) -> p (a g) q", q=P)
            wsT = sb("wsT", [P, GROUPS, P])
            z_gain = sb("z_gain", [P, SG])
        bank = [ctx.enter_context(nc.psum_tensor(f"{tag}_bank{i}", [P, BANK], F32)) for i in range(8)]
        x_in = [sem(f"{tag}_x_in{i}") for i in range(2)]
        x_sq = sem(f"{tag}_x_sq")
        x_norm = sem(f"{tag}_x_norm")
        x_rstd = sem(f"{tag}_x_rstd")
        z_var = sem(f"{tag}_z_var")
        passed = sem(f"{tag}_passed")
        z_rstd = sem(f"{tag}_z_rstd")
        ob_rstd = sem(f"{tag}_ob_rstd")
        xr_free = sem(f"{tag}_xr_free")
        piece_t = sem(f"{tag}_piece_t")
        piece_full = sem(f"{tag}_piece_full")
        piece_lo = sem(f"{tag}_piece_lo")
        w_loaded = [sem(f"{tag}_w_loaded{i}") for i in range(2)]
        w_hi_ok = sem(f"{tag}_w_hi_ok")
        w_split = sem(f"{tag}_w_split")
        w_free = [sem(f"{tag}_w_free{i}") for i in range(2)]
        hT_free = sem(f"{tag}_hT_free")
        bank_free = [sem(f"{tag}_bank_free{i}") for i in range(GB)]
        product = sem(f"{tag}_product")
        staged = [sem(f"{tag}_staged{i}") for i in range(4)]
        stored = [sem(f"{tag}_stored{i}") for i in range(4)]
        dve_link = sem(f"{tag}_dve_link")
        pool_link = sem(f"{tag}_pool_link")
        gelu_ok = sem(f"{tag}_gelu_ok")
        zn_ok = sem(f"{tag}_zn_ok")
        gelu_used = sem(f"{tag}_gelu_used")
        mixed = sem(f"{tag}_mixed")
        mix_free = sem(f"{tag}_mix_free")
        ob_ok = sem(f"{tag}_ob_ok")
        ob_sq = sem(f"{tag}_ob_sq")
        ws_in = sem(f"{tag}_ws_in")
        ws_t = sem(f"{tag}_ws_t")
        ws_ok = sem(f"{tag}_ws_ok")
        block = ctx.enter_context(nc.Block())

        def split_slot(c, j):
            return 2 * c + j

        @block.sync
        def _(sp):
            if gmlp:
                sp.dma_start(ws_raw[:, :, :], io["w_s"][0].rearrange("g p q -> p g q")).then_inc(ws_in, 16)
                sp.dma_start(z_gain[:, :], io["gmlp_norm"].rearrange("a d -> (a d)").partition_broadcast(P)
                             ).then_inc(ws_in, 16)
            with each(sp, n_super) as s:
                def load_w(c):
                    for j in range(2):
                        n = split_slot(c, j)
                        sp.wait_ge(w_split, s * 2 * len(blocks) + n + 1)
                        a = col_at[blocks[c]]
                        sp.dma_start(w_raw[:, j], w_in[j, :, :, a:a + BANK]).then_inc(w_loaded[j], 16)
                for t in range(tiles):
                    sp.wait_ge(x_norm, s * tiles + t + 1)
                    sp.dma_start(xin[:, t % 2], x_rows[s, t]).then_inc(x_in[t % 2], 16)
                    if t == 1:
                        load_w(0)
                for c in range(len(blocks)):
                    if c + 1 < len(blocks):
                        load_w(c + 1)
                    for i, n in enumerate(stores):
                        if groups[n][0] == c:
                            _, name, a, h = groups[n]
                            slot = i % 4
                            sp.wait_ge(staged[slot], s * (len(stores) // 4) + i // 4 + 1)
                            dst = out[name][s, a, :, h * NB:(h + 1) * NB] if name in "qk" else out[name][s, a]
                            sp.dma_start(dst, stage[:, slot, 0:dst.shape[-1]]).then_inc(stored[slot], 16)
            for slot in range(4):
                sp.wait_ge(stored[slot], 16 + 16 * n_super * len(stores[slot::4]))

        @block.gpsimd
        def _(pool):
            def rstd(dst, src):
                pool_n[0] += 1
                pool.tensor_tensor(dst, src, keep["eps"][:, :], ALU.add).then_inc(pool_link, 1)
                pool.wait_ge(pool_link, s * POOL_LINKS + pool_n[0])
                return pool.tensor_tensor(dst, dst, keep["minus_half"][:, :], ALU.pow)
            pool_n = [0]
            with each(pool, n_super) as s:
                for t in range(tiles):
                    pool.wait_ge(x_sq, s * tiles + t + 1)
                    rstd(stat[:, 1, t:t + 1], stat[:, 0, t:t + 1]).then_inc(x_rstd, 1)
                for a in range(tiles if gmlp else 0):
                    pool.wait_ge(z_var, s * tiles + a + 1)
                    rstd(stat[:, 3, 2:3], stat[:, 3, 1:2]).then_inc(z_rstd, 1)
                for a in range(tiles if gmlp else 0):
                    pool.wait_ge(ob_sq, s * tiles + a + 1)
                    rstd(stat[:, 6, a:a + 1], stat[:, 4, a:a + 1]).then_inc(ob_rstd, 1)

        def stage_slot(eng, s, n):
            i = stores.index(n)
            eng.wait_ge(stored[i % 4], (s * (len(stores) // 4) + i // 4 + 1) * 16)
            return i % 4

        @block.scalar
        def _(act):
            with each(act, n_super) as s:
                def split(c, j):
                    n = split_slot(c, j)
                    act.wait_ge(w_loaded[j], (s * len(blocks) + c + 1) * 16)
                    act.wait_ge(w_free[c % 2], s * W_USES[c % 2] + c // 2 + 1)
                    act.activation(w_hi[:, c % 2, j * HALF_K:(j + 1) * HALF_K, :], w_raw[:, j],
                                   ACT.Copy).then_inc(w_hi_ok, 1)
                split(0, 0)
                split(0, 1)
                for pair in range(PAIRS):
                    for t in (2 * pair, 2 * pair + 1):
                        act.wait_ge(x_in[t % 2], (s * PAIRS + pair + 1) * 16)
                        act.wait_ge(xr_free, s * tiles + t + 1)
                        act.activation(xr[:, t % 2], xin[:, t % 2], ACT.Square, scale=float(D) ** -0.5,
                                       accum_out=stat[:, 0, t:t + 1]).then_inc(x_sq, 1)
                    for kh in range(2):
                        n = 2 * pair + kh
                        act.wait_ge(piece_t, s * NP + n + 1)
                        act.wait_ge(piece_lo, s * NP + n + 1)
                        for i in range(HALF_K):
                            k = kh * HALF_K + i
                            b = bank[2 * (n % 3) + i // 2]
                            act.activation(h_full[:, n % 2, i], b[:, (i % 2) * 256:(i % 2) * 256 + 256],
                                           ACT.Identity, scale=gain[:, k:k + 1], bias=shift[:, k:k + 1]
                                           ).then_inc(piece_full, 1)
                        act.wait_ge(piece_full, (s * NP + n + 1) * HALF_K)
                        for b in (2 * (n % 3), 2 * (n % 3) + 1):
                            act.sem_inc(bank_free[b], 1)
                for n, (c, name, a, h) in enumerate(groups):
                    if name in "quz":
                        act.wait_ge(product, s * NG + n + 1)
                        b = n % GB
                        if name == "q":
                            slot = stage_slot(act, s, n)
                            act.activation(stage[:, slot, 0:NB], bank[b][:, 0:NB], ACT.Copy,
                                           scale=float(DH) ** -0.5).then_inc(staged[slot], 1)
                            act.wait_ge(staged[slot], s * (len(stores) // 4) + stores.index(n) // 4 + 1)
                            act.sem_inc(bank_free[b], 1)
                        else:
                            m = [g for g in range(len(groups)) if groups[g][1] in "uz"].index(n)
                            act.wait_ge(gelu_used, s * 2 * tiles + m + 1)
                            act.activation(act_out[:, m % 2], bank[b][:, :], ACT.Gelu_apprx_tanh
                                           ).then_inc(gelu_ok, 1)
                            act.wait_ge(gelu_ok, s * 2 * tiles + m + 1)
                            act.sem_inc(bank_free[b], 1)
                        if name == "u":
                            act.wait_ge(ob_ok, s * tiles + a + 1)
                            act.activation(zn[:, :], spatial[:, a], ACT.Square,
                                           scale=float(SG) ** -0.5, accum_out=stat[:, 4, a:a + 1]).then_inc(ob_sq, 1)
                    if c + 1 < len(blocks) and n - first[c] in (1, 3):
                        split(c + 1, (n - first[c]) // 2)

        @block.vector
        def _(dve):
            dve.sem_inc(x_norm, 2)
            dve.sem_inc(xr_free, 2)
            dve.sem_inc(piece_lo, 2)
            dve.sem_inc(w_split, 2)
            dve.sem_inc(hT_free, 1)
            for slot in range(4):
                dve.sem_inc(stored[slot], 16)
            dve.sem_inc(w_free[0], 1)
            dve.sem_inc(w_free[1], 1)
            for b in range(GB):
                dve.sem_inc(bank_free[b], 1)
            if gmlp:
                dve.sem_inc(gelu_used, 2)
                dve.sem_inc(mix_free, 2)
                for g in range(2):
                    dve.wait_ge(ws_t, g + 1)
                    dve.tensor_copy(wsT[:, 4 * g:4 * g + 4, :].rearrange("p g q -> p (g q)"),
                                    bank[6 + g][:, :]).then_inc(ws_ok, 1)
                dve.wait_ge(ws_in, 32)
            with each(dve, n_super) as s:
                link = Chain(dve, dve_link, s * DVE_LINKS)

                def split(c, j):
                    n = split_slot(c, j)
                    dve.wait_ge(w_hi_ok, s * 2 * len(blocks) + n + 1)
                    half = slice(j * HALF_K, (j + 1) * HALF_K)
                    dve.tensor_tensor(w_lo[:, c % 2, half, :], w_raw[:, j],
                                      w_hi[:, c % 2, half, :].bitcast(F32), ALU.subtract
                                      ).then_inc(w_split, 1)
                def spatial_out(a):
                    dve.wait_ge(mixed, s * tiles + a + 2)
                    dve.tensor_tensor(
                        spatial[:, a].rearrange("p (g d) -> p g d", g=GROUPS),
                        bank[6 + a % 2][:, :].rearrange("p (g d) -> p g d", g=GROUPS),
                        keep["small"][:, SMALL["b_s"][0]:SMALL["b_s"][1], None].broadcast_to([P, GROUPS, GD]),
                        ALU.add).then_inc(mix_free, 1)
                split(0, 0)
                split(0, 1)
                for pair in range(PAIRS):
                    for t in (2 * pair, 2 * pair + 1):
                        dve.wait_ge(x_rstd, s * tiles + t + 1)
                        dve.tensor_scalar(xr[:, t % 2], xin[:, t % 2], stat[:, 1, t:t + 1], None,
                                          ALU.mult).then_inc(x_norm, 1)
                    for kh in range(2):
                        n = 2 * pair + kh
                        dve.wait_ge(piece_full, (s * NP + n + 1) * HALF_K)
                        if n == 0:
                            dve.wait_ge(hT_free, s + 1)
                        ks = slice(kh * HALF_K, (kh + 1) * HALF_K)
                        cols = slice(pair * 2 * P, (pair + 1) * 2 * P)
                        link(dve.tensor_copy(hT_hi[:, ks, cols], h_full[:, n % 2]))
                        dve.tensor_tensor(hT_lo[:, ks, cols], h_full[:, n % 2],
                                          hT_hi[:, ks, cols].bitcast(F32), ALU.subtract
                                          ).then_inc(piece_lo, 1)
                for n, (c, name, a, h) in enumerate(groups):
                    b = n % GB
                    if name in "kv":
                        dve.wait_ge(product, s * NG + n + 1)
                        slot = stage_slot(dve, s, n)
                        w = NB if name == "k" else BANK
                        dve.tensor_copy(stage[:, slot, 0:w], bank[b][:, 0:w]).then_inc(staged[slot], 1)
                        dve.wait_ge(staged[slot], s * (len(stores) // 4) + stores.index(n) // 4 + 1)
                        dve.sem_inc(bank_free[b], 1)
                    if name == "z":
                        dve.wait_ge(gelu_ok, s * 2 * tiles + a + 1)
                        z = act_out[:, a % 2]
                        link(dve.bn_stats(stat[:, 2, 0:6], z))
                        apart(dve, passed)
                        dve.bn_aggr(stat[:, 3, 0:2], stat[:, 2, 0:6]).then_inc(z_var, 1)
                        if a >= 1:
                            spatial_out(a - 1)
                        dve.wait_ge(z_rstd, s * tiles + a + 1)
                        link(dve.tensor_scalar(zn[:, :], z, stat[:, 3, 0:1], stat[:, 3, 2:3],
                                               ALU.subtract, ALU.mult))
                        dve.sem_inc(gelu_used, 1)
                        dve.tensor_tensor(zn[:, :], zn[:, :], z_gain[:, :], ALU.mult).then_inc(zn_ok, 1)
                    if name == "u":
                        if a == 0:
                            spatial_out(tiles - 1)
                        dve.wait_ge(gelu_ok, s * 2 * tiles + tiles + a + 1)
                        dve.wait_ge(mix_free, s * tiles + tiles + 2)
                        dve.tensor_tensor(spatial[:, a], spatial[:, a], act_out[:, a % 2],
                                          ALU.mult).then_inc(ob_ok, 1)
                        dve.wait_ge(ob_ok, s * tiles + a + 1)
                        dve.sem_inc(gelu_used, 1)
                        dve.wait_ge(ob_rstd, s * tiles + a + 1)
                        slot = stage_slot(dve, s, n)
                        link(dve.tensor_scalar(stage[:, slot, :], spatial[:, a], stat[:, 6, a:a + 1], None,
                                               ALU.mult))
                        dve.sem_inc(staged[slot], 1)
                    if c + 1 < len(blocks) and n - first[c] in (1, 3):
                        split(c + 1, (n - first[c]) // 2)
                assert link.n == DVE_LINKS, (link.n, DVE_LINKS)

        @block.tensor
        def _(pe):
            if gmlp:
                pe.sem_inc(mixed, 1)
                pe.wait_ge(ws_in, 32)
                for g in range(GROUPS):
                    t = pe.transpose(bank[6 + g // 4][:, (g % 4) * P:(g % 4 + 1) * P], ws_raw[:, g, :],
                                     keep["ident"][:, :])
                    if g % 4 == 3:
                        t.then_inc(ws_t, 1)
                pe.wait_ge(ws_ok, 2)
            with each(pe, n_super) as s:
                for pair in range(PAIRS):
                    for kh in range(2):
                        n = 2 * pair + kh
                        for b, before in uses[n]:
                            pe.wait_ge(bank_free[b], s * seen[b] + before + 1)
                        pe.wait_ge(x_norm, s * tiles + 2 * pair + 4)
                        for i in range(HALF_K):
                            k = kh * HALF_K + i
                            for j in range(2):
                                a = (i % 2) * 256 + j * P
                                t = pe.transpose(bank[2 * (n % 3) + i // 2][:, a:a + P],
                                                 xr[:, j, k * P:(k + 1) * P], keep["ident"][:, :])
                        t.then_inc(piece_t, 1)
                    pe.wait_ge(piece_t, s * NP + 2 * pair + 2)
                    pe.sem_inc(xr_free, 2)

                def mix(a):
                    pe.wait_ge(zn_ok, s * tiles + a + 1)
                    pe.wait_ge(mix_free, s * tiles + a + 1)
                    for g in range(GROUPS):
                        mm = pe.matmul(bank[6 + a % 2][:, g * GD:(g + 1) * GD], wsT[:, g, :],
                                       zn[:, g * GD:(g + 1) * GD], start=True, stop=True)
                    mm.then_inc(mixed, 1)

                pe.wait_ge(piece_lo, (s + 1) * NP + 2)
                for n, (c, name, a, h) in enumerate(groups):
                    if n == first[c]:
                        pe.wait_ge(w_split, s * 2 * len(blocks) + 2 * c + 4)
                    (b, before), = uses[NP + n]
                    pe.wait_ge(bank_free[b], s * seen[b] + before + 1)
                    wh, wl = w_hi[:, c % 2], w_lo[:, c % 2]
                    for k in range(KD):
                        for x, (hp, wp) in enumerate(((hT_hi, wh), (hT_lo, wh), (hT_hi, wl))):
                            if name in "qk":
                                mm = pe.matmul(bank[b][:, 0:NB], wp[:, k, a * P:(a + 1) * P],
                                               hp[:, k, h * NB:(h + 1) * NB],
                                               start=(k == 0 and x == 0), stop=(k == KD - 1 and x == 2))
                            else:
                                mm = pe.matmul(bank[b][:, :], hp[:, k, a * P:(a + 1) * P], wp[:, k, :],
                                               start=(k == 0 and x == 0), stop=(k == KD - 1 and x == 2))
                    mm.then_inc(product, 1)
                    if name == "z" and a >= 1:
                        mix(a - 1)
                    if name == "u" and a == 0:
                        mix(tiles - 1)
                    if n == last[c]:
                        pe.wait_ge(product, s * NG + n + 1)
                        pe.sem_inc(w_free[c % 2], 1)
                pe.sem_inc(hT_free, 1)

def attention_phase(nc, sem, io, scratch, keep):
    N = HEADS * BLOCKS
    PIECES = 4
    KP, QP = (SEQ + CTX) // PIECES, SEQ // PIECES
    INTERIOR = EDGE
    LAG_EXP, LAG_T, LAG_PV, LAG_O = 1, 2, 3, 4

    def local_rows(j):
        if j < EDGE:
            return 0, WIN_H
        if j >= BLOCKS - EDGE:
            return ROWS - WIN_H, WIN_H
        return 2 * j - WIN_H // 2, KEY_ROWS

    VARIANTS = [INTERIOR] + list(range(EDGE)) + list(range(BLOCKS - EDGE, BLOCKS))

    def variant(j):
        return VARIANTS.index(j) if j in VARIANTS else 0

    with ExitStack() as ctx:
        def sb(name, shape, dt=F32):
            return ctx.enter_context(nc.sbuf_tensor(f"att_{name}", shape, dt))

        k_raw = sb("k_raw", [P, SEQ + CTX])
        q_raw = sb("q_raw", [P, SEQ])
        k_hi = sb("k_hi", [P, 2, SEQ + CTX], F32R)
        k_lo = sb("k_lo", [P, 2, SEQ + CTX], F32R)
        q_parts = sb("q_parts", [P, 2, SEQ], F32R)
        v_sb = sb("v", [P, 2, TILES + CTX // P, DH])
        bias = sb("bias", [P, 2, len(VARIANTS), KEYS])
        neg_s = sb("neg_s", [P, 3, KEYS])
        probs = sb("probs", [P, 3, KEYS])
        probsT = sb("probsT", [P, 2, 7, P])
        low = sb("low", [P, 4])
        total = sb("total", [P, 4])
        inv = sb("inv", [P, 4])
        ps_s = [ctx.enter_context(nc.psum_tensor(f"ps_s{i}", [P, 2 * BANK], F32)) for i in range(2)]
        ps_ta = ctx.enter_context(nc.psum_tensor("ps_ta", [P, BANK], F32))
        ps_tb = ctx.enter_context(nc.psum_tensor("ps_tb", [P, BANK], F32))
        ps_o = [ctx.enter_context(nc.psum_tensor(f"ps_o{i}", [P, BANK], F32)) for i in range(2)]

        k_in = sem("att_k_in")
        q_in = sem("att_q_in")
        v_in = [sem(f"att_v_in{i}") for i in range(2)]
        bias_in = [sem(f"att_bias_in{i}") for i in range(2)]
        bias_ok = sem("att_bias_ok")
        rounded = sem("att_rounded")
        split_ok = sem("att_split_ok")
        scored = sem("att_scored")
        biased = sem("att_biased")
        exped = sem("att_exped")
        turned = sem("att_turned")
        turned_a = sem("att_turned_a")
        turned_b = sem("att_turned_b")
        summed = sem("att_summed")
        inverted = sem("att_inverted")
        w_out_in = sem("att_w_out_in")
        pool_passed = sem("att_pool_passed")
        dve_passed = sem("att_dve_passed")
        sp_passed = sem("att_sp_passed")
        output = sem("att_output")
        block = ctx.enter_context(nc.Block())
        kT, kTc = scratch["kT"], scratch["kTc"]
        qT = scratch["qT"]
        v_rows = scratch["v"].rearrange("(t p) n -> p t n", p=P)
        vc_rows = scratch["vc"].rearrange("(t p) n -> p t n", p=P)

        @block.sync
        def _(sp):
            def load(head, done, par):
                rows = bass.ds(head * DH, DH)
                if done is not None:
                    sp.wait_ge(split_ok, (done + 1) * 2 * PIECES)
                for half in range(2):
                    part = slice(half * DH, (half + 1) * DH)
                    sp.dma_start(k_raw[part, 0:SEQ], kT[rows, :]).then_inc(k_in, 16)
                    sp.dma_start(k_raw[part, SEQ:SEQ + CTX], kTc[rows, :]).then_inc(k_in, 16)
                    sp.dma_start(q_raw[part, :], qT[rows, :]).then_inc(q_in, 16)
                if done is not None:
                    sp.wait_ge(summed, done * BLOCKS + 2)
                    apart(sp, sp_passed)
                cols = bass.ds(head * DH, DH)
                sp.dma_start(v_sb[:, par, 0:TILES, :], v_rows[:, :, cols]).then_inc(v_in[par], 16)
                sp.dma_start(v_sb[:, par, TILES:, :], vc_rows[:, :, cols]).then_inc(v_in[par], 16)
                if done is not None:
                    sp.wait_ge(biased, done * BLOCKS + 2)
                for v, j in enumerate(VARIANTS):
                    base, rows_n = local_rows(j)
                    slot = base - 2 * j + WIN_H - 1
                    src = scratch["table"].rearrange("p h m k -> h p (m k)")[head]
                    sp.dma_start(bias[:, par, v, 0:rows_n * GRID_W],
                                 src[:, slot * GRID_W:(slot + rows_n) * GRID_W]).then_inc(bias_in[par], 16)
            load(0, None, 0)
            with sp.Fori(0, HEADS // 2) as i:
                for par in range(2):
                    load((i * 2 + par + 1) % HEADS, i * 2 + par, 1 - par)
            sp.wait_ge(v_in[0], 32 * (HEADS // 2 + 1))

        BIAS_OK0 = 2 * len(VARIANTS)

        @block.gpsimd
        def _(pool):
            for par in range(2):
                for v, j in enumerate(VARIANTS):
                    n = local_rows(j)[1] * GRID_W
                    pool.memset(bias[:, par, v, n:n + CTX], 0.0).then_inc(bias_ok, 1)

            def mask(par, n, nth):
                pool.wait_ge(bias_in[par], 16 * len(VARIANTS) * nth)
                pool.wait_ge(bias_ok, BIAS_OK0 + 2 * n - 2)
                apart(pool, pool_passed)
                pool.memset(bias[0:GRID_W, par, 0, WIN_H * GRID_W:LOCAL], MASKED).then_inc(bias_ok, 1)
                pool.wait_ge(bias_ok, BIAS_OK0 + 2 * n - 1)
                apart(pool, pool_passed)
                pool.memset(bias[GRID_W:P, par, 0, 0:GRID_W], MASKED).then_inc(bias_ok, 1)
            mask(0, 1, 1)
            pool.dma_start(keep["w_out"][:, :, :], io["w_out"][0].rearrange("(k p) n -> p k n", p=P)
                           ).then_inc(w_out_in, 16)
            with pool.Fori(0, HEADS // 2) as i:
                for par in range(2):
                    mask(1 - par, i * 2 + par + 2, i + 1 + par)
            pool.wait_ge(w_out_in, 16)

        @block.scalar
        def _(act):
            def split(par, head, p):
                if p < PIECES:
                    act.wait_ge(k_in, (head + 1) * 64)
                    act.activation(k_hi[:, par, p * KP:(p + 1) * KP], k_raw[:, p * KP:(p + 1) * KP],
                                   ACT.Copy).then_inc(rounded, 1)
                else:
                    p -= PIECES
                    act.wait_ge(q_in, (head + 1) * 32)
                    act.activation(q_parts[:, par, p * QP:(p + 1) * QP], q_raw[:, p * QP:(p + 1) * QP],
                                   ACT.Copy).then_inc(rounded, 1)
            for p in range(2 * PIECES):
                split(0, 0, p)
            with act.Fori(0, HEADS // 2) as i:
                for n in range(2 * BLOCKS + LAG_O):
                    par, j = n // BLOCKS, n % BLOCKS
                    if 2 <= j < 2 + 2 * PIECES and n < 2 * BLOCKS:
                        split(1 - par, i * 2 + par + 1, j - 2)
                    m = n - LAG_EXP
                    if 0 <= m < 2 * BLOCKS:
                        w = local_rows(m % BLOCKS)[1] * GRID_W + CTX
                        act.wait_ge(biased, i * 2 * BLOCKS + m + 3)
                        act.wait_ge(turned, i * 2 * BLOCKS + m + 1)
                        act.activation(probs[:, m % 3, 0:w], neg_s[:, m % 3, 0:w], ACT.Exp, scale=-1.0,
                                       bias=low[:, m % 4:m % 4 + 1],
                                       accum_out=total[:, m % 4:m % 4 + 1]).then_inc(exped, 1)
                    m = n - LAG_T
                    if 0 <= m < 2 * BLOCKS:
                        act.wait_ge(turned, i * 2 * BLOCKS + m + 4)
                        act.wait_ge(summed, i * 2 * BLOCKS + m + 1)
                        act.activation(probsT[:, m % 2, 0:4, :].rearrange("p c q -> p (c q)"), ps_ta[:, :],
                                       ACT.Copy).then_inc(turned_a, 1)

        @block.vector
        def _(dve):
            def split(par, head, p):
                dve.wait_ge(rounded, head * 2 * PIECES + p + 1)
                if p < PIECES:
                    cols = slice(p * KP, (p + 1) * KP)
                    dve.tensor_tensor(k_lo[:, par, cols], k_raw[:, cols], k_hi[:, par, cols].bitcast(F32),
                                      ALU.subtract).then_inc(split_ok, 1)
                else:
                    cols = slice((p - PIECES) * QP, (p - PIECES + 1) * QP)
                    low_half = q_parts[DH:P, par, cols]
                    dve.tensor_tensor(low_half, q_raw[DH:P, cols], low_half.bitcast(F32),
                                      ALU.subtract).then_inc(split_ok, 1)
            for s, v in ((biased, 2), (exped, 3), (turned, 3), (turned_a, 1), (turned_b, 1), (summed, 2),
                         (output, 2)):
                dve.sem_inc(s, v)
            for p in range(2 * PIECES):
                split(0, 0, p)
            with dve.Fori(0, HEADS // 2) as i:
                at = i * 2 * BLOCKS
                for n in range(2 * BLOCKS + LAG_O):
                    par, j = n // BLOCKS, n % BLOCKS
                    if n < 2 * BLOCKS:
                        w = local_rows(j)[1] * GRID_W + CTX
                        if j == 0:
                            dve.wait_ge(bias_ok, BIAS_OK0 + (i * 2 + par + 1) * 2)
                        dve.wait_ge(scored, at + n + 1)
                        dve.wait_ge(exped, at + n + 1)
                        apart(dve, dve_passed)
                        dve.tensor_tensor_reduce(neg_s[:, n % 3, 0:w], ps_s[n % 2][:, 2 * BANK - w:],
                                                 bias[:, par, variant(j), 0:w], -1.0, -MASKED, ALU.add,
                                                 ALU.min, low[:, n % 4:n % 4 + 1]).then_inc(biased, 1)
                        if 2 <= j < 2 + 2 * PIECES:
                            split(1 - par, i * 2 + par + 1, j - 2)
                    m = n - LAG_T
                    if 0 <= m < 2 * BLOCKS:
                        inner = local_rows(m % BLOCKS)[1] > WIN_H
                        a = 4 if inner else 5
                        dve.wait_ge(turned, at + m + 4)
                        dve.wait_ge(summed, at + m + 1)
                        dve.tensor_copy(probsT[:, m % 2, a:, :].rearrange("p c q -> p (c q)"),
                                        ps_tb[:, (a - 4) * P:3 * P]).then_inc(turned_b, 1)
                        dve.reciprocal(inv[:, m % 4:m % 4 + 1], total[:, m % 4:m % 4 + 1]).then_inc(inverted, 1)
                    m = n - LAG_O
                    if 0 <= m < 2 * BLOCKS:
                        dve.wait_ge(summed, at + m + 3)
                        dve.wait_ge(inverted, at + m + 1)
                        dve.tensor_scalar(
                            keep["o_a"][:, m % BLOCKS, bass.ds((i * 2 + m // BLOCKS) * DH, DH)],
                            ps_o[m % 2][:, 0:DH], inv[:, m % 4:m % 4 + 1], None, ALU.mult).then_inc(output, 1)

        @block.tensor
        def _(pe):
            with pe.Fori(0, HEADS // 2) as i:
                at = i * 2 * BLOCKS
                for n in range(2 * BLOCKS + LAG_PV):
                    if n < 2 * BLOCKS:
                        par, j = n // BLOCKS, n % BLOCKS
                        base, rows = local_rows(j)
                        if j == 0:
                            pe.wait_ge(split_ok, (i * 2 + par + 1) * 2 * PIECES)
                        pe.wait_ge(biased, at + n + 1)
                        k0 = base * GRID_W
                        first = (rows - 4) * GRID_W
                        for dst, src, width in ((BANK - first, k0, first), (BANK, k0 + first, CTX),
                                                (BANK + CTX, SEQ, CTX)):
                            for x, part in enumerate((k_hi, k_lo)):
                                mm = pe.matmul(ps_s[n % 2][:, dst:dst + width],
                                               q_parts[:, par, j * P:(j + 1) * P],
                                               part[:, par, src:src + width], start=(x == 0), stop=(x == 1))
                        mm.then_inc(scored, 1)
                    m = n - LAG_T
                    if 0 <= m < 2 * BLOCKS:
                        rows = local_rows(m % BLOCKS)[1]
                        local = rows * GRID_W
                        pe.wait_ge(exped, at + m + 4)
                        pe.wait_ge(turned_a, at + m + 1)
                        pe.wait_ge(turned_b, at + m + 1)
                        for c in range(4):
                            pe.transpose(ps_ta[:, c * P:(c + 1) * P], probs[:, m % 3, c * P:(c + 1) * P],
                                         keep["ident"][:, :])
                        if rows > WIN_H:
                            pe.transpose(ps_tb[:, 0:P], probs[:, m % 3, 4 * P:5 * P], keep["ident"][:, :])
                        for c in range(2):
                            t = pe.transpose(ps_tb[:, (c + 1) * P:(c + 2) * P],
                                             probs[:, m % 3, local + c * P:local + (c + 1) * P],
                                             keep["ident"][:, :])
                        t.then_inc(turned, 1)
                    m = n - LAG_PV
                    if 0 <= m < 2 * BLOCKS:
                        par, j = m // BLOCKS, m % BLOCKS
                        base, rows = local_rows(j)
                        if j == 0:
                            pe.wait_ge(v_in[par], (i + 1) * 32)
                        pe.wait_ge(turned_a, at + m + 2)
                        pe.wait_ge(turned_b, at + m + 2)
                        pe.wait_ge(output, at + m + 1)
                        chunks = [(c, base // 2 + c, P) for c in range(4)]
                        if rows > WIN_H:
                            chunks.append((4, base // 2 + 4, GRID_W))
                        chunks += [(5, TILES, P), (6, TILES + 1, P)]
                        for c, tile, n_keys in chunks:
                            mm = pe.matmul(ps_o[m % 2][:, 0:DH], probsT[0:n_keys, m % 2, c, :],
                                           v_sb[0:n_keys, par, tile, :], start=(c == 0), stop=(c == 6))
                        mm.then_inc(summed, 1)

def pipeline(eng, count, depth, step):
    for n in range(depth):
        step(n, n % 2, lambda l, n=n: 0 <= n - l < count)
    with eng.Fori(0, (count - depth) // 2) as i:
        for p in range(2):
            step(i * 2 + depth + p, (depth + p) % 2, lambda l: True)
    for n in range(count, count + depth):
        step(n, n % 2, lambda l, n=n: 0 <= n - l < count)


def mixing_phase(nc, sem, io, scratch, keep):
    LAGS = 6
    with ExitStack() as ctx:
        def sb(name, shape, dt=F32):
            return ctx.enter_context(nc.sbuf_tensor(f"mix_{name}", shape, dt))

        w_hi = sb("w_hi", [P, KD, D], F32R)
        w_lo = sb("w_lo", [P, KD, D], F32R)
        router = sb("router", [P, KD, EXPERTS])
        gate_row = sb("gate_row", [P, D])
        xin = sb("xin", [P, 2, D])
        o_b = sb("o_b", [P, 2, SG])
        o_an = sb("o_an", [P, NA])
        oT_hi = sb("oT_hi", [P, 2, KD, P], F32R)
        oT_lo = sb("oT_lo", [P, 2, KD, P], F32R)
        x_new = sb("x_new", [P, 2, D])
        x_norm = sb("x_norm", [P, 2, D])
        hT = sb("hT", [P, 2, KD, P])
        junk_o = sb("junk_o", [P, NA])
        junk_x = sb("junk_x", [P, D])
        stat = sb("stat", [P, 8, 2])
        soft = sb("soft", [P, 2, EXPERTS])
        ps_o = ctx.enter_context(nc.psum_tensor("ps_oT", [P, 2 * BANK], F32))
        ps_m = [ctx.enter_context(nc.psum_tensor(f"ps_mix{i}", [P, BANK], F32)) for i in range(2)]
        ps_x = ctx.enter_context(nc.psum_tensor("ps_xT", [P, 2 * BANK], F32))
        ps_l = ctx.enter_context(nc.psum_tensor("ps_logit", [P, BANK], F32))

        w_rounded = sem("mix_w_rounded")
        w_ok = sem("mix_w_ok")
        const_in = sem("mix_const_in")
        tile_in = [sem(f"mix_tile_in{i}") for i in range(2)]
        o_sq = sem("mix_o_sq")
        o_rstd = sem("mix_o_rstd")
        o_normed = sem("mix_o_normed")
        o_turned = sem("mix_o_turned")
        o_rounded = sem("mix_o_rounded")
        o_split = sem("mix_o_split")
        mixed = sem("mix_mixed")
        gated = sem("mix_gated")
        added = sem("mix_added")
        x_sq = sem("mix_x_sq")
        x_rstd = sem("mix_x_rstd")
        x_normed = sem("mix_x_normed")
        x_turned = sem("mix_x_turned")
        h_ok = sem("mix_h_ok")
        routed = sem("mix_routed")
        top_ok = sem("mix_top_ok")
        exped = sem("mix_exped")
        pool_link = sem("mix_pool_link")
        recip = sem("mix_recip")
        stored = [sem(f"mix_stored{i}") for i in range(2)]
        aff_ok = sem("mix_aff_ok")
        block = ctx.enter_context(nc.Block())
        w_raw = keep["w_out"]
        x_rows = io["x"][0].rearrange("(t p) n -> t p n", p=P)
        ob_rows = scratch["o_b"].rearrange("(t p) n -> t p n", p=P)
        new_rows = scratch["x_new"].rearrange("(t p) n -> t p n", p=P)
        norm_rows = scratch["x_norm"].rearrange("(t p) n -> t p n", p=P)
        out_gain = keep["small"][:, SMALL["out_norm_a"][0]:SMALL["out_norm_b"][1]]

        @block.sync
        def _(sp):
            sp.dma_start(gate_row[:, :], scratch["mod"][0, 2 * D:3 * D].partition_broadcast(P)
                         ).then_inc(const_in, 16)
            sp.dma_start(router[:, :, :], io["w_router"][0].rearrange("(k p) e -> p k e", p=P)
                         ).then_inc(const_in, 16)
            with sp.Fori(0, TILES // 2) as i:
                for par in range(2):
                    sp.wait_ge(added, i * 2 + par + 1)
                    sp.dma_start(o_b[:, par], ob_rows[i * 2 + par]).then_inc(tile_in[par], 16)
                    sp.dma_start(xin[:, par], x_rows[i * 2 + par]).then_inc(tile_in[par], 16)

        @block.gpsimd
        def _(pool):
            def rstd(dst, src, n):
                pool.tensor_tensor(dst, src, keep["eps"][:, :], ALU.add).then_inc(pool_link, 1)
                pool.wait_ge(pool_link, n)
                return pool.tensor_tensor(dst, dst, keep["minus_half"][:, :], ALU.pow)

            def step(t, par, active):
                if active(0):
                    pool.wait_ge(o_sq, t + 1)
                    n = 1 if isinstance(t, int) and t == 0 else t * 2
                    rstd(stat[:, 1, par:par + 1], stat[:, 0, par:par + 1], n).then_inc(o_rstd, 1)
                if active(2):
                    pool.wait_ge(x_normed, t - 1)
                    pool.dma_start(new_rows[t - 2], x_new[:, par]).then_inc(stored[par], 16)
                    pool.dma_start(norm_rows[t - 2], x_norm[:, par]).then_inc(stored[par], 16)
                if active(1):
                    q = 1 - par
                    pool.wait_ge(x_sq, t)
                    n = t * 2 + 1 if active(0) else TILES * 2
                    rstd(stat[:, 3, q:q + 1], stat[:, 2, q:q + 1], n).then_inc(x_rstd, 1)
            pipeline(pool, TILES, LAGS, step)
            for s in stored:
                pool.wait_ge(s, 16 * TILES)

        @block.scalar
        def _(act):
            for c in range(KD):
                act.activation(w_hi[:, c, :], w_raw[:, c, :], ACT.Copy,
                               scale=out_gain[:, c:c + 1]).then_inc(w_rounded, 1)

            def step(t, par, active):
                if active(0):
                    if not (isinstance(t, int) and t == 0):
                        act.wait_ge(o_rstd, t)
                    act.activation(junk_o[:, :], keep["o_a"][:, t, :], ACT.Square, scale=float(NA) ** -0.5,
                                   accum_out=stat[:, 0, par:par + 1]).then_inc(o_sq, 1)
                q = 1 - par
                if active(3):
                    act.wait_ge(x_turned, t - 2)
                    act.wait_ge(routed, t - 2)
                    for k in range(KD):
                        act.activation(hT[:, q, k], ps_x[:, k * P:(k + 1) * P], ACT.Identity,
                                       scale=keep["gain2"][:, k:k + 1], bias=keep["shift2"][:, k:k + 1]
                                       ).then_inc(h_ok, 1)
                if active(5):
                    act.wait_ge(top_ok, t - 4)
                    act.activation(soft[:, q], ps_l[:, 0:EXPERTS], ACT.Exp, bias=stat[:, 4, q:q + 1],
                                   accum_out=stat[:, 5, q:q + 1]).then_inc(exped, 1)
                if active(1):
                    act.wait_ge(added, t + 2)
                    if not (isinstance(t, int) and t == 1):
                        act.wait_ge(x_sq, t - 1)
                    act.activation(junk_x[:, :], x_new[:, q], ACT.Square, scale=float(D) ** -0.5,
                                   accum_out=stat[:, 2, q:q + 1]).then_inc(x_sq, 1)
            pipeline(act, TILES, LAGS, step)

        @block.vector
        def _(dve):
            dve.sem_inc(added, 2)
            dve.sem_inc(routed, 2)
            for c in range(KD):
                dve.wait_ge(w_rounded, c + 1)
                dve.scalar_tensor_tensor(out=w_lo[:, c, :], in0=w_raw[:, c, :],
                                         scalar=out_gain[:, c:c + 1], in1=w_hi[:, c, :].bitcast(F32),
                                         op0=ALU.mult, op1=ALU.subtract).then_inc(w_ok, 1)
            dve.wait_ge(const_in, 32)

            def step(t, par, active):
                q = 1 - par

                def gate(half):
                    cols = slice(half * BANK, (half + 1) * BANK)
                    dve.wait_ge(mixed, t * 2 - 1 + half)
                    dve.tensor_tensor(x_new[:, q, cols], ps_m[half][:, :], gate_row[:, cols],
                                      ALU.mult).then_inc(gated, 1)
                if active(5):
                    dve.wait_ge(routed, t - 2)
                    dve.tensor_reduce(stat[:, 4, q:q + 1], ps_l[:, 0:EXPERTS], AX.X, ALU.max,
                                      negate=True).then_inc(top_ok, 1)
                if active(2):
                    dve.wait_ge(x_rstd, t - 1)
                    if not (isinstance(t, int) and t < 4):
                        dve.wait_ge(stored[par], (t - 2 - par) * 16)
                    dve.tensor_scalar(x_norm[:, par], x_new[:, par], stat[:, 3, par:par + 1], None,
                                      ALU.mult).then_inc(x_normed, 1)
                if active(0):
                    dve.wait_ge(o_rstd, t + 1)
                    dve.tensor_scalar(o_an[:, :], keep["o_a"][:, t, :], stat[:, 1, par:par + 1], None,
                                      ALU.mult).then_inc(o_normed, 1)
                if active(1):
                    dve.wait_ge(tile_in[q], (t - 1 - q) * 16 + 32)
                    if not (isinstance(t, int) and t < 3):
                        dve.wait_ge(stored[q], (t - 1 - q) * 16)
                    gate(0)
                if active(0):
                    dve.wait_ge(o_turned, t + 1)
                    oT = ps_o[:, :].rearrange("p (k t) -> p k t", t=P)
                    dve.tensor_copy(oT_hi[:, par], oT).then_inc(o_rounded, 1)
                    dve.wait_ge(o_rounded, t + 1)
                    dve.tensor_tensor(oT_lo[:, par], oT, oT_hi[:, par].bitcast(F32), ALU.subtract
                                      ).then_inc(o_split, 1)
                if active(6):
                    dve.wait_ge(exped, t - 5)
                    dve.reciprocal(stat[:, 6, par:par + 1], stat[:, 5, par:par + 1]).then_inc(recip, 1)
                    dve.wait_ge(recip, t - 5)
                    dve.tensor_scalar(keep["aff"][:, :, t - 6], soft[:, par], stat[:, 6, par:par + 1], None,
                                      ALU.mult).then_inc(aff_ok, 1)
                if active(1):
                    gate(1)
                    dve.wait_ge(gated, t * 2)
                    dve.tensor_tensor(x_new[:, q], x_new[:, q], xin[:, q], ALU.add).then_inc(added, 1)
            pipeline(dve, TILES, LAGS, step)

        @block.tensor
        def _(pe):
            ident = keep["ident"]

            def mix(t, q, half):
                cols = slice(half * BANK, (half + 1) * BANK)
                if not (isinstance(t, int) and t == 1):
                    pe.wait_ge(gated, t * 2 - 3 + half)
                for k in range(KD):
                    for x, (o, w) in enumerate(((oT_hi, w_hi), (oT_lo, w_hi), (oT_hi, w_lo))):
                        mm = pe.matmul(ps_m[half][:, :], o[:, q, k, :], w[:, k, cols],
                                       start=(k == 0 and x == 0), stop=(k == KD - 1 and x == 2))
                mm.then_inc(mixed, 1)

            def step(t, par, active):
                if active(1):
                    if isinstance(t, int) and t == 1:
                        pe.wait_ge(w_ok, KD)
                    pe.wait_ge(o_split, t)
                    mix(t, 1 - par, 0)
                if active(0):
                    pe.wait_ge(tile_in[par], (t - par) * 16 + 32)
                    pe.wait_ge(o_normed, t + 1)
                    for k in range(KD):
                        src = o_an[:, k * P:(k + 1) * P] if k < KNA else o_b[:, par, (k - KNA) * P:(k - KNA + 1) * P]
                        tr = pe.transpose(ps_o[:, k * P:(k + 1) * P], src, ident[:, :])
                    tr.then_inc(o_turned, 1)
                if active(1):
                    mix(t, 1 - par, 1)
                if active(2):
                    pe.wait_ge(x_normed, t - 1)
                    if not (isinstance(t, int) and t == 2):
                        pe.wait_ge(h_ok, (t - 2) * KD)
                    for k in range(KD):
                        tr = pe.transpose(ps_x[:, k * P:(k + 1) * P], x_norm[:, par, k * P:(k + 1) * P],
                                          ident[:, :])
                    tr.then_inc(x_turned, 1)
                if active(4):
                    pe.wait_ge(h_ok, (t - 3) * KD)
                    if not (isinstance(t, int) and t == 4):
                        pe.wait_ge(exped, t - 4)
                    for k in range(KD):
                        mm = pe.matmul(ps_l[:, 0:EXPERTS], hT[:, par, k, :], router[:, k, :],
                                       start=(k == 0), stop=(k == KD - 1))
                    mm.then_inc(routed, 1)
            pipeline(pe, TILES, LAGS, step)

BITS = 30
DIGIT = 2
ROUNDS = BITS // DIGIT
TRIALS = 2 ** DIGIT - 1
UNROLL = 5


def expert_phase(nc, sem, io, scratch, keep):
    U = 18
    PAIRS = 6
    FC = 2 * P
    RAW, SPLIT, AHEAD = 6, 3, 2
    HALVES = CAP // P
    VALS = 5
    w_gate = io["w_gate"][0].rearrange("e (k p) (u n) -> e u p k n", p=P, n=FC)
    w_up = io["w_up"][0].rearrange("e (k p) (u n) -> e u p k n", p=P, n=FC)
    w_down = io["w_down"][0].rearrange("e (u k p) n -> e u p k n", p=P, k=FC // P)
    with ExitStack() as ctx:
        def sb(name, shape, dt=F32):
            return ctx.enter_context(nc.sbuf_tensor(f"moe_{name}", shape, dt))

        raw = sb("raw", [P, RAW, KD * FC])
        w_hi = sb("w_hi", [P, SPLIT, KD * FC], F32R)
        w_lo = sb("w_lo", [P, SPLIT, KD * FC], F32R)
        xs = sb("xs", [P, HALVES, D])
        xs_full = sb("xs_full", [P, KD, CAP])
        xT_hi = sb("xT_hi", [P, KD, CAP], F32R)
        xT_lo = sb("xT_lo", [P, KD, CAP], F32R)
        silu_g = sb("silu_g", [P, 2, 2 * CAP])
        g_full = sb("g_full", [P, 2, 2 * CAP])
        g_hi = sb("g_hi", [P, PAIRS, 2 * CAP], F32R)
        g_lo = sb("g_lo", [P, PAIRS, 2 * CAP], F32R)
        y = sb("y", [P, HALVES, D])
        gate_row = sb("gate_row", [P, D])
        ones_b = sb("ones_b", [P, P], BF16)
        upto_b = sb("upto_b", [P, P], BF16)
        place = sb("place", [P, ROUNDS * TRIALS], U32)
        digit = sb("digit", [P, ROUNDS * TRIALS], U32)
        digits = sb("digits", [P, ROUNDS * TRIALS], U32)
        cut = sb("cut", [P, EXPERTS])
        trial = sb("trial", [P, TRIALS, EXPERTS])
        kept = sb("kept", [P, TRIALS, EXPERTS])
        best = sb("best", [P, EXPERTS])
        reached = sb("reached", [P, TILES, TRIALS, EXPERTS], BF16)
        need = sb("need", [P, EXPERTS])
        above_b = sb("above_b", [P, EXPERTS, TILES], BF16)
        equal_b = sb("equal_b", [P, EXPERTS, TILES], BF16)
        picked_b = sb("picked_b", [P, EXPERTS, TILES], BF16)
        slot_of = sb("slot_of", [P, EXPERTS, TILES])
        iota_i = sb("iota_i", [P, CAP], U32)
        slot_row = sb("slot_row", [P, CAP], BF16)
        vals = sb("vals", [P, EXPERTS, TILES, VALS], BF16)
        rest = sb("rest", [P, EXPERTS, TILES])
        aff_rest = sb("aff_rest", [P, EXPERTS, TILES])
        tile_i = sb("tile_i", [P, TILES], U32)
        part = sb("part", [P, 1], U32)
        one_hot = sb("one_hot", [P, TILES, CAP], BF16)
        pick = sb("pick", [P, HALVES, VALS])
        pick_sum = sb("pick_sum", [P, HALVES])
        idx_next = sb("idx_next", [P, HALVES], U32)
        idx_now = sb("idx_now", [P, HALVES], U32)
        gate_next = sb("gate_next", [P, HALVES])
        gate_now = sb("gate_now", [P, HALVES])
        bank = [ctx.enter_context(nc.psum_tensor(f"moe_bank{i}", [P, BANK], F32)) for i in range(8)]

        w_in = [sem(f"moe_w_in{i}") for i in range(RAW)]
        w_rounded = sem("moe_w_rounded")
        w_split = sem("moe_w_split")
        product = sem("moe_product")
        silu_ok = sem("moe_silu_ok")
        g_ok = sem("moe_g_ok")
        g_rounded = sem("moe_g_rounded")
        g_split = sem("moe_g_split")
        xs_in = sem("moe_xs_in")
        xs_turned = sem("moe_xs_turned")
        xs_ok = sem("moe_xs_ok")
        x_rounded = sem("moe_x_rounded")
        x_split = sem("moe_x_split")
        y_ok = sem("moe_y_ok")
        y_added = sem("moe_y_added")
        hot_ok = sem("moe_hot_ok")
        picked = sem("moe_picked")
        idx_ok = sem("moe_idx_ok")
        idx_kept = sem("moe_idx_kept")
        row_in = sem("moe_row_in")
        consts = sem("moe_consts")
        passed = sem("moe_passed")
        pool_own = sem("moe_pool_own")
        chain = sem("moe_chain")
        vals_ok = sem("moe_vals_ok")
        marked = sem("moe_marked")
        counted = sem("moe_counted")
        rank_in = sem("moe_rank_in")
        ranked = sem("moe_ranked")
        dve_own = sem("moe_dve_own")
        block = ctx.enter_context(nc.Block())

        def next_expert(e, u):
            return (e, u + AHEAD) if u + AHEAD < U else (e + 1, u + AHEAD - U)

        @block.sync
        def _(sp):
            sp.dma_start(gate_row[:, :], scratch["mod"][0, 5 * D:6 * D].partition_broadcast(P)
                         ).then_inc(row_in, 16)

            def load(expert, n, u):
                sp.wait_ge(w_split, n * U + u + 1)
                src = w_down[expert, u - 2 * PAIRS] if u >= 2 * PAIRS else (w_gate, w_up)[u % 2][expert, u // 2]
                dst = raw[:, u % RAW].rearrange("p (k n) -> p k n", n=src.shape[-1])
                sp.dma_start(dst, src).then_inc(w_in[u % RAW], 16)
            with sp.Fori(0, EXPERTS) as e:
                for u in range(U):
                    load(e, e, u)
            for u in range(AHEAD):
                load(0, EXPERTS, u)

        @block.gpsimd
        def _(pool):
            pool.iota(place[:, :], pattern=[[-DIGIT, ROUNDS], [0, TRIALS]], base=BITS - DIGIT,
                      channel_multiplier=0).then_inc(consts, 1)
            pool.iota(digit[:, :], pattern=[[0, ROUNDS], [1, TRIALS]], base=1,
                      channel_multiplier=0).then_inc(consts, 1)
            pool.memset(ones_b[:, :], 1.0).then_inc(consts, 1)
            own = Chain(pool, pool_own)
            pool.wait_ge(consts, 3)
            own(pool.affine_select(out=upto_b[:, :], in_=ones_b[:, :], compare_op=ALU.is_ge, fill=0.0, base=0,
                                   pattern=[[1, P]], channel_multiplier=-1))
            own(pool.iota(iota_i[:, :], pattern=[[1, CAP]], base=1, channel_multiplier=0))
            own(pool.iota(tile_i[:, :], pattern=[[1, TILES]], base=0, channel_multiplier=0))
            own(pool.iota(part[:, :], pattern=[[0, 1]], base=0, channel_multiplier=1))
            own(pool.tensor_copy(slot_row[:, :], iota_i[:, :]))
            wide = [P, EXPERTS, TILES]
            aff = keep["aff"]
            own(pool.tensor_copy(vals[:, :, :, 0], part[:, :, None].broadcast_to(wide)))
            own(pool.tensor_copy(vals[:, :, :, 1], tile_i[:, None, :].broadcast_to(wide)))
            own(pool.tensor_copy(vals[:, :, :, 2], aff[:, :, :]))
            own(pool.tensor_tensor(aff_rest[:, :, :], aff[:, :, :], vals[:, :, :, 2], ALU.subtract))
            own(pool.tensor_copy(vals[:, :, :, 3], aff_rest[:, :, :]))
            pool.tensor_tensor(vals[:, :, :, 4], aff_rest[:, :, :], vals[:, :, :, 3], ALU.subtract
                               ).then_inc(vals_ok, 1)

            def gather(n, before=None):
                if before is not None:
                    pool.wait_ge(xs_turned, before + 1)
                pool.wait_ge(idx_ok, n + 1)
                apart(pool, passed)
                for m in range(HALVES):
                    pool.indirect_dma_start(
                        out=xs[:, m, :], out_offset=None, in_=scratch["x_norm"],
                        in_offset=bass.IndirectOffsetOnAxis(ap=idx_next[:, m:m + 1], axis=0)
                    ).then_inc(xs_in, 16)
            gather(0)
            with pool.Fori(0, EXPERTS) as e:
                pool.wait_ge(idx_ok, e + 1)
                apart(pool, passed)
                pool.tensor_copy(idx_now[:, :], idx_next[:, :]).then_inc(idx_kept, 1)
                gather(e + 1, e)
                pool.wait_ge(y_ok, e * 4 + 8)
                pool.wait_ge(idx_kept, e + 1)
                apart(pool, passed)
                for m in range(HALVES):
                    pool.indirect_dma_start(
                        out=scratch["x_new"],
                        out_offset=bass.IndirectOffsetOnAxis(ap=idx_now[:, m:m + 1], axis=0),
                        in_=y[:, m, :], in_offset=None, compute_op=ALU.add).then_inc(y_added, 16)
                pool.wait_ge(y_added, (e + 1) * 16 * HALVES)
            pool.wait_ge(xs_in, (EXPERTS + 1) * 16 * HALVES)

        @block.scalar
        def _(act):
            def split(n, u):
                act.wait_ge(w_in[u % RAW], (n * (U // RAW) + u // RAW + 1) * 16)
                act.wait_ge(product, n * U + u + 1)
                act.activation(w_hi[:, u % SPLIT], raw[:, u % RAW], ACT.Copy).then_inc(w_rounded, 1)

            def modulate(n):
                act.wait_ge(xs_turned, n + 1)
                for k in range(KD):
                    act.activation(xs_full[:, k], bank[k // 2][:, (k % 2) * CAP:(k % 2 + 1) * CAP],
                                   ACT.Identity, scale=keep["gain2"][:, k:k + 1],
                                   bias=keep["shift2"][:, k:k + 1]).then_inc(xs_ok, 1)
            for u in range(AHEAD):
                split(0, u)
            modulate(0)
            with act.Fori(0, EXPERTS) as e:
                for u in range(U):
                    split(*next_expert(e, u))
                    if u % 2 and u < 2 * PAIRS:
                        i = u // 2
                        act.wait_ge(product, e * U + u + 3)
                        act.wait_ge(g_ok, e * PAIRS + i + 1)
                        act.activation(silu_g[:, i % 2], bank[i % 2][:, :], ACT.Silu).then_inc(silu_ok, 1)
                    if u % 2 == 0 and 2 <= u <= 2 * PAIRS:
                        i = u // 2 - 1
                        act.wait_ge(g_ok, e * PAIRS + i + 3)
                        act.activation(g_hi[:, i], g_full[:, i % 2], ACT.Copy).then_inc(g_rounded, 1)
                    if u == 14:
                        modulate(e + 1)

        @block.vector
        def _(dve):
            for s, v in ((w_split, RAW), (product, SPLIT), (silu_ok, 2), (g_ok, 2), (y_ok, 4)):
                dve.sem_inc(s, v)
            own = Chain(dve, chain)

            def split(n, u):
                dve.wait_ge(w_rounded, n * U + u + 1)
                dve.tensor_tensor(w_lo[:, u % SPLIT], raw[:, u % RAW], w_hi[:, u % SPLIT].bitcast(F32),
                                  ALU.subtract).then_inc(w_split, 1)

            aff = keep["aff"]
            dve.wait_ge(consts, 2)
            own(dve.tensor_tensor(digits[:, :], digit[:, :], place[:, :], ALU.logical_shift_left))
            own(dve.memset(cut[:, :], 0.0))
            before = own.n
            tries = [P, TILES, TRIALS, EXPERTS]
            with dve.Fori(0, ROUNDS // UNROLL) as i:
                for r in (i * UNROLL + n for n in range(UNROLL)):
                    step = Chain(dve, chain, before + r * 4)
                    digit_of = digits[:, bass.ds(r * TRIALS, TRIALS)]
                    step(dve.tensor_tensor(trial[:, :, :].bitcast(U32),
                                           cut[:, None, :].bitcast(U32).broadcast_to([P, TRIALS, EXPERTS]),
                                           digit_of[:, :, None].broadcast_to([P, TRIALS, EXPERTS]), ALU.bitwise_or))
                    dve.tensor_tensor(reached[:, :, :, :],
                                      aff[:, :, :].rearrange("p e t -> p t e")[:, :, None, :].broadcast_to(tries),
                                      trial[:, None, :, :].broadcast_to(tries), ALU.is_ge).then_inc(marked, 1)
                    dve.wait_ge(counted, r + 1)
                    step(dve.scalar_tensor_tensor(
                        out=kept[:, :, :], in0=bank[0][:, 0:TRIALS * EXPERTS].rearrange("p (j e) -> p j e", j=TRIALS),
                        scalar=CAP - 0.5, in1=trial[:, :, :], op0=ALU.is_ge, op1=ALU.mult))
                    step(dve.tensor_reduce(best[:, :], kept[:, :, :].rearrange("p j e -> p e j"), AX.X, ALU.max))
                    step(dve.tensor_tensor(cut[:, :], cut[:, :], best[:, :], ALU.max))
            own = Chain(dve, chain, before + ROUNDS * 4)
            wide = cut[:, :, None].broadcast_to([P, EXPERTS, TILES])
            dve.tensor_tensor(above_b[:, :, :], aff[:, :, :], wide, ALU.is_gt).then_inc(marked, 1)
            dve.tensor_tensor(equal_b[:, :, :], aff[:, :, :], wide, ALU.is_equal).then_inc(rank_in, 1)
            dve.wait_ge(counted, ROUNDS + 1)
            own(dve.tensor_scalar(need[:, :], bank[0][:, 0:EXPERTS], -1.0, float(CAP), ALU.mult, ALU.add))
            dve.wait_ge(ranked, 1)
            own(dve.tensor_tensor(rest[:, :, :], bank[1][:, 0:EXPERTS * TILES].rearrange("p (e t) -> p e t", t=TILES),
                                  need[:, :, None].broadcast_to([P, EXPERTS, TILES]), ALU.is_le))
            own(dve.tensor_tensor(rest[:, :, :], rest[:, :, :], equal_b[:, :, :], ALU.mult))
            dve.tensor_tensor(picked_b[:, :, :], rest[:, :, :], above_b[:, :, :], ALU.add).then_inc(rank_in, 1)
            dve.wait_ge(ranked, 2)
            own(dve.tensor_tensor(slot_of[:, :, :], bank[1][:, 0:EXPERTS * TILES].rearrange("p (e t) -> p e t", t=TILES),
                                  picked_b[:, :, :], ALU.mult))
            dve.wait_ge(vals_ok, 1)

            def hot(expert, t):
                dve.tensor_scalar(one_hot[:, t], slot_row[:, :],
                                  slot_of[:, expert, t:t + 1] if isinstance(expert, int)
                                  else slot_of[:, bass.ds(expert, 1), t], None, ALU.is_equal
                                  ).then_inc(hot_ok, 1)

            def take(n, link):
                dve.wait_ge(picked, n + 1)
                link(dve.tensor_copy(pick[:, :, :], bank[4][:, 0:HALVES * 8].rearrange(
                    "p (m v) -> p m v", v=8)[:, :, 0:VALS]))
                dve.scalar_tensor_tensor(out=idx_next[:, :], in0=pick[:, :, 1], scalar=float(P),
                                         in1=pick[:, :, 0], op0=ALU.mult, op1=ALU.add).then_inc(idx_ok, 1)
                link(dve.tensor_tensor(pick_sum[:, :], pick[:, :, 2], pick[:, :, 3], ALU.add))
                link(dve.tensor_tensor(gate_next[:, :], pick_sum[:, :], pick[:, :, 4], ALU.add))

            def split_tokens(n):
                dve.wait_ge(xs_ok, (n + 1) * KD)
                dve.tensor_copy(xT_hi[:, :, :], xs_full[:, :, :]).then_inc(x_rounded, 1)
                dve.wait_ge(x_rounded, n + 1)
                dve.tensor_tensor(xT_lo[:, :, :], xs_full[:, :, :], xT_hi[:, :, :].bitcast(F32), ALU.subtract
                                  ).then_inc(x_split, 1)
            for t in range(TILES):
                hot(0, t)
            take(0, own)
            for u in range(AHEAD):
                split(0, u)
            split_tokens(0)
            dve.wait_ge(row_in, 16)
            LINKS = 4
            with dve.Fori(0, EXPERTS) as e:
                link = Chain(dve, dve_own, e * LINKS)
                for u in range(U):
                    split(*next_expert(e, u))
                    if u == 0:
                        dve.wait_ge(y_ok, e * 4 + 4)
                        link(dve.tensor_copy(gate_now[:, :], gate_next[:, :]))
                    if u < 4:
                        if u == 0:
                            dve.wait_ge(picked, e + 1)
                        for t in range(4 * u, 4 * u + 4):
                            hot((e + 1) % EXPERTS, t)
                    if u == 8:
                        dve.wait_ge(idx_kept, e + 1)
                        take(e + 1, link)
                    if u % 2 == 0 and 2 <= u <= 2 * PAIRS:
                        i = u // 2 - 1
                        dve.wait_ge(product, e * U + u + 3)
                        dve.wait_ge(silu_ok, e * PAIRS + i + 3)
                        dve.tensor_tensor(g_full[:, i % 2], bank[2 + i % 2][:, :], silu_g[:, i % 2], ALU.mult
                                          ).then_inc(g_ok, 1)
                    if u % 2 and 3 <= u <= 2 * PAIRS + 1:
                        i = (u - 3) // 2
                        dve.wait_ge(g_rounded, e * PAIRS + i + 1)
                        dve.tensor_tensor(g_lo[:, i], g_full[:, i % 2], g_hi[:, i].bitcast(F32), ALU.subtract
                                          ).then_inc(g_split, 1)
                    if u == 15:
                        split_tokens(e + 1)
                dve.wait_ge(product, e * U + U + 3)
                for m in range(HALVES):
                    for half in range(2):
                        cols = slice(half * BANK, (half + 1) * BANK)
                        dve.scalar_tensor_tensor(out=y[:, m, cols], in0=bank[4 + 2 * m + half][:, :],
                                                 scalar=gate_now[:, m:m + 1], in1=gate_row[:, cols],
                                                 op0=ALU.mult, op1=ALU.mult).then_inc(y_ok, 1)
                assert link.n == LINKS

        @block.tensor
        def _(pe):
            ident = keep["ident"]
            pe.wait_ge(consts, 3)
            pe.wait_ge(pool_own, 1)
            with pe.Fori(0, ROUNDS // UNROLL) as i:
                for r in (i * UNROLL + n for n in range(UNROLL)):
                    pe.wait_ge(marked, r + 1)
                    for t in range(TILES):
                        mm = pe.matmul(bank[0][:, 0:TRIALS * EXPERTS], ones_b[:, :],
                                       reached[:, t, :, :].rearrange("p j e -> p (j e)"),
                                       start=(t == 0), stop=(t == TILES - 1))
                    mm.then_inc(counted, 1)
            pe.wait_ge(marked, ROUNDS + 1)
            for t in range(TILES):
                mm = pe.matmul(bank[0][:, 0:EXPERTS], ones_b[:, :], above_b[:, :, t],
                               start=(t == 0), stop=(t == TILES - 1))
            mm.then_inc(counted, 1)
            for r, marks in enumerate((equal_b, picked_b)):
                pe.wait_ge(rank_in, r + 1)
                rank = bank[1][:, 0:EXPERTS * TILES].rearrange("p (e t) -> p e t", t=TILES)
                for d in range(TILES - 1, 0, -1):
                    pe.matmul(rank[:, :, d:], ones_b[:, :], marks[:, :, 0:TILES - d],
                              start=(d == TILES - 1), stop=False, skip_group_check=True)
                mm = pe.matmul(rank, upto_b[:, :], marks[:, :, :], start=False, stop=True,
                               skip_group_check=True)
                mm.then_inc(ranked, 1)

            def take(expert, n):
                pe.wait_ge(hot_ok, (n + 1) * TILES)
                for m in range(HALVES):
                    for t in range(TILES):
                        row = (vals[:, expert, t, :] if isinstance(expert, int)
                               else vals[:, bass.ds(expert, 1), t, :].rearrange("p a v -> p (a v)"))
                        mm = pe.matmul(bank[4][:, m * 8:m * 8 + VALS], one_hot[:, t, m * P:(m + 1) * P], row,
                                       start=(t == 0), stop=(t == TILES - 1))
                mm.then_inc(picked, 1)

            def turn(n):
                pe.wait_ge(xs_in, (n + 1) * 16 * HALVES)
                for k in range(KD):
                    for m in range(HALVES):
                        a = (k % 2) * CAP + m * P
                        tr = pe.transpose(bank[k // 2][:, a:a + P], xs[:, m, k * P:(k + 1) * P], ident[:, :])
                tr.then_inc(xs_turned, 1)
            take(0, 0)
            turn(0)
            with pe.Fori(0, EXPERTS) as e:
                for u in range(U):
                    if u == 7:
                        pe.wait_ge(y_ok, e * 4 + 4)
                        take((e + 1) % EXPERTS, e + 1)
                    if u == 13:
                        pe.wait_ge(g_ok, (e + 1) * PAIRS + 2)
                        turn(e + 1)
                    if u == 0:
                        pe.wait_ge(x_split, e + 1)
                    pe.wait_ge(w_split, e * U + u + 1 + RAW)
                    wh, wl = w_hi[:, u % SPLIT], w_lo[:, u % SPLIT]
                    if u < 2 * PAIRS:
                        i = u // 2
                        pe.wait_ge(g_ok if u % 2 else silu_ok, e * PAIRS + i + 1)
                        b = bank[i % 2 + 2 * (u % 2)]
                        for j in range(2):
                            for k in range(KD):
                                cols = slice(k * FC + j * P, k * FC + (j + 1) * P)
                                for x, (w, h) in enumerate(((wh, xT_hi), (wh, xT_lo), (wl, xT_hi))):
                                    mm = pe.matmul(b[:, j * CAP:(j + 1) * CAP], w[:, cols], h[:, k, :],
                                                   start=(k == 0 and x == 0), stop=(k == KD - 1 and x == 2))
                    else:
                        i = u - 2 * PAIRS
                        if i == 0:
                            pe.wait_ge(idx_ok, e + 2)
                        pe.wait_ge(g_split, e * PAIRS + i + 1)
                        for j in range(2):
                            for m in range(HALVES):
                                toks = slice(j * CAP + m * P, j * CAP + (m + 1) * P)
                                for half in range(2):
                                    cols = slice(j * D + half * BANK, j * D + (half + 1) * BANK)
                                    for x, (g, w) in enumerate(((g_hi, wh), (g_lo, wh), (g_hi, wl))):
                                        mm = pe.matmul(bank[4 + 2 * m + half][:, :], g[:, i, toks], w[:, cols],
                                                       start=(i == 0 and j == 0 and x == 0),
                                                       stop=(i == PAIRS - 1 and j == 1 and x == 2))
                    mm.then_inc(product, 1)


def final_phase(nc, sem, io, scratch, keep, out):
    with ExitStack() as ctx:
        def sb(name, shape, dt=F32):
            return ctx.enter_context(nc.sbuf_tensor(f"fin_{name}", shape, dt))

        RING = 8
        x = sb("x", [P, RING, D])
        junk = sb("junk", [P, RING, D])
        gain = sb("gain", [P, D])
        stat = sb("stat", [P, RING, 2])
        gain_in = sem("fin_gain_in")
        x_in = [sem(f"fin_x_in{i}") for i in range(RING)]
        squared = sem("fin_squared")
        pool_own = sem("fin_pool_own")
        rooted = sem("fin_rooted")
        scaled = sem("fin_scaled")
        stored = [sem(f"fin_stored{i}") for i in range(RING)]
        block = ctx.enter_context(nc.Block())
        x_rows = scratch["x_new"].rearrange("(i t p) n -> i t p n", p=P, t=RING)
        out_rows = out[0].rearrange("(i t p) n -> i t p n", p=P, t=RING)
        STEPS = TILES // RING

        @block.sync
        def _(sp):
            sp.dma_start(gain[:, :], io["norm_final"].partition_broadcast(P)).then_inc(gain_in, 16)
            with sp.Fori(0, STEPS) as i:
                for t in range(RING):
                    sp.wait_ge(stored[t], (i + 1) * 16)
                    sp.dma_start(x[:, t], x_rows[i, t]).then_inc(x_in[t], 16)

        @block.scalar
        def _(act):
            for s in stored:
                act.sem_inc(s, 16)

            def store(i, t):
                act.wait_ge(scaled, i * RING + t + 1)
                act.dma_start(out_rows[i, t], x[:, t]).then_inc(stored[t], 16)
            with act.Fori(0, STEPS) as i:
                for t in range(RING):
                    act.wait_ge(x_in[t], (i + 1) * 16)
                    act.activation(junk[:, t], x[:, t], ACT.Square, scale=float(D) ** -0.5,
                                   accum_out=stat[:, t, 0:1]).then_inc(squared, 1)
                    if t >= 2:
                        store(i, t - 2)
                store(i, RING - 2)
                store(i, RING - 1)
            for s in stored:
                act.wait_ge(s, 16 * (STEPS + 1))

        @block.gpsimd
        def _(pool):
            with pool.Fori(0, STEPS) as i:
                for t in range(RING):
                    pool.wait_ge(squared, i * RING + t + 1)
                    pool.tensor_tensor(stat[:, t, 1:2], stat[:, t, 0:1], keep["eps"][:, :], ALU.add).then_inc(pool_own, 1)
                    pool.wait_ge(pool_own, i * RING + t + 1)
                    pool.tensor_tensor(stat[:, t, 1:2], stat[:, t, 1:2], keep["minus_half"][:, :], ALU.pow
                                       ).then_inc(rooted, 1)

        @block.vector
        def _(dve):
            dve.wait_ge(gain_in, 16)
            with dve.Fori(0, STEPS) as i:
                for t in range(RING):
                    dve.wait_ge(rooted, i * RING + t + 1)
                    dve.scalar_tensor_tensor(out=x[:, t], in0=x[:, t], scalar=stat[:, t, 1:2], in1=gain[:, :],
                                             op0=ALU.mult, op1=ALU.mult).then_inc(scaled, 1)

def hybrid_layer_kernel(nc, io, out):
    with ExitStack() as ctx:
        taken = []

        def sem(name):
            taken.append(nc.alloc_semaphore(name))
            return taken[-1]

        def phase(build, *args):
            build(nc, sem, *args)
            nc.clear_and_free_semaphores(taken)
            nc.all_engine_barrier()
            taken.clear()

        def sb(name, shape):
            return ctx.enter_context(nc.sbuf_tensor(name, shape, F32))

        def dram(name, shape):
            return nc.dram_tensor(name, shape, F32, kind="Internal").ap()

        scratch = {
            "mod": dram("mod_dram", (2, N_MOD * D)),
            "rel": dram("rel_dram", (HEADS * RPB_H, GRID_W, 2 * GRID_W)),
            "table": dram("table_dram", (P, HEADS, SLOTS, GRID_W)),
            "qT": dram("qT_dram", (NA, SEQ)),
            "kT": dram("kT_dram", (NA, SEQ)),
            "v": dram("v_dram", (SEQ, NA)),
            "kTc": dram("kTc_dram", (NA, CTX)),
            "vc": dram("vc_dram", (CTX, NA)),
            "o_b": dram("o_b_dram", (SEQ, SG)),
            "x_new": dram("x_new_dram", (SEQ, D)),
            "x_norm": dram("x_norm_dram", (SEQ, D)),
        }
        keep = {"ident": sb("ident", [P, P]), "small": sb("small", [P, SMALL_ROWS]),
                "minus_half": sb("minus_half", [P, 1]), "eps": sb("eps", [P, 1]), "aff": sb("aff", [P, EXPERTS, TILES])}
        for name in "1c2":
            keep["gain" + name] = sb("gain" + name, [P, KD])
            keep["shift" + name] = sb("shift" + name, [P, KD])

        def columns(a, steps):
            return a.rearrange("(a p) (s n) -> s a p n", p=P, s=steps)

        def rows(a, steps):
            return a.rearrange("(s a p) n -> s a p n", p=P, s=steps)

        phase(modulation_phase, io, scratch, keep)
        phase(projection_phase, io, keep, "ctx", rows(io["ctx"][0], 1), 1, CTX // P, "kv",
              keep["gainc"], keep["shiftc"],
              {"k": columns(scratch["kTc"], 1), "v": rows(scratch["vc"], 1)})
        phase(projection_phase, io, keep, "tok", rows(io["x"][0], 2), 2, TILES // 2, "qkvzu",
              keep["gain1"], keep["shift1"],
              {"q": columns(scratch["qT"], 2), "k": columns(scratch["kT"], 2),
               "v": rows(scratch["v"], 2), "u": rows(scratch["o_b"], 2)})
        with nc.sbuf_tensor("o_a", [P, TILES, NA], F32) as o_a, nc.sbuf_tensor("w_out", [P, KD, D], F32) as w_out:
            keep["o_a"], keep["w_out"] = o_a, w_out
            phase(attention_phase, io, scratch, keep)
            phase(mixing_phase, io, scratch, keep)
        phase(expert_phase, io, scratch, keep)
        final_phase(nc, sem, io, scratch, keep, out)


_INS = ["x", "c", "ctx", "c_ctx", "w_mod", "b_mod", "norm1", "w_in", "rpb", "w_s", "b_s", "gmlp_norm",
        "out_norm_a", "out_norm_b", "w_out", "norm2", "w_router", "w_gate", "w_up", "w_down", "norm_final"]
_OUTS = [((1, SEQ, D), "float32")]


def kernel(**inputs):
    import numpy as _np
    import concourse.bacc as _bacc
    from concourse import mybir as _mybir
    from concourse.bass_utils import run_bass_kernel_spmd as _run

    nc = _bacc.Bacc("TRN2", target_bir_lowering=False, num_devices=1)
    arrays, io = {}, {}
    for name in _INS:
        a = _np.ascontiguousarray(inputs[name])
        arrays[f"in_{name}_dram"] = a
        io[name] = nc.dram_tensor(f"in_{name}_dram", a.shape, _mybir.dt.from_np(a.dtype), kind="ExternalInput").ap()
    outs = []
    for i, (shape, dtype) in enumerate(_OUTS):
        dt = _mybir.dt.from_np(_np.dtype(dtype))
        outs.append(nc.dram_tensor(f"out_{i}_dram", shape, dt, kind="ExternalOutput").ap())
    hybrid_layer_kernel(nc, io, outs[0])
    r = _run(nc, [arrays], core_ids=[0])
    got = tuple(r.results[0][f"out_{i}_dram"] for i in range(len(_OUTS)))
    return got[0]
```

```python
from contextlib import ExitStack

import concourse.bass as bass
from concourse import mybir

F32 = mybir.dt.float32
F32R = mybir.dt.float32r
BF16 = mybir.dt.bfloat16
U32 = mybir.dt.uint32
ALU = mybir.AluOpType
ACT = mybir.ActivationFunctionType
AX = mybir.AxisListType

P = 128
D = 1024
KD = D // P
SEQ = 2048
CTX = 256
TILES = SEQ // P
GRID_W = 64
ROWS = SEQ // GRID_W
HEADS = 8
DH = 64
NA = HEADS * DH
KNA = NA // P
WIN_H = 8
WIN_W = 16
RPB_H = 2 * WIN_H - 1
RPB_W = 2 * WIN_W - 1
SG = D - NA
GROUPS = 8
GD = SG // GROUPS
N_MOD = 6
EXPERTS = 16
CAP = 2 * SEQ // EXPERTS
DE = 1536
EPS = 1e-6
EARLY = 2
MASKED = -1e30
BANK = 512

SMALL = {}
for _name, _rows in (("c", KD), ("c_ctx", KD), ("norm1", KD), ("norm2", KD),
                     ("out_norm_a", KNA), ("out_norm_b", KNA), ("b_s", GROUPS),
                     ("b_mod", N_MOD * KD)):
    SMALL[_name] = (sum(b - a for a, b in SMALL.values()), sum(b - a for a, b in SMALL.values()) + _rows)
SMALL_ROWS = max(b for _, b in SMALL.values())

KEY_ROWS = WIN_H + 1
SLOTS = RPB_H + 1
LOCAL = KEY_ROWS * GRID_W
KEYS = LOCAL + CTX
BLOCKS = ROWS // 2
EDGE = 2


def key_base(j):
    return min(max(2 * j - WIN_H // 2, 0), ROWS - KEY_ROWS)


class Chain:

    def __init__(self, eng, sem, base=0):
        self.eng, self.sem, self.base, self.n = eng, sem, base, 0

    def __call__(self, instruction):
        instruction.then_inc(self.sem, 1)
        self.n += 1
        self.eng.wait_ge(self.sem, self.base + self.n)


def apart(eng, passed):
    eng.sem_inc(passed, 1)


def each(eng, n):
    from contextlib import nullcontext
    return eng.Fori(0, n) if n > 1 else nullcontext(0)


def modulation_phase(nc, sem, io, scratch, keep):
    UNITS = EARLY * D // BANK
    COLS = EARLY * KD
    w_mod = io["w_mod"][0].rearrange("(k p) (u n) -> u p k n", p=P, n=BANK)
    with ExitStack() as ctx:
        def sb(name, shape, dt=F32):
            return ctx.enter_context(nc.sbuf_tensor(f"m_{name}", shape, dt))

        small_rows = sb("small_rows", [SMALL_ROWS, P])
        cond = keep["cond"]
        wm = sb("wm", [P, UNITS, KD, BANK])
        mod_rows = sb("mod_rows", [2, EARLY * D])
        mod_cols = sb("mod_cols", [P, COLS, 2])
        rel = sb("rel", [GRID_W, HEADS * RPB_H, 2 * GRID_W])
        ps_t = ctx.enter_context(nc.psum_tensor("ps_t", [P, BANK], F32))
        ps_m = [ctx.enter_context(nc.psum_tensor(f"ps_m{i}", [P, BANK], F32)) for i in range(2)]
        small_in = sem("small_in")
        wm_in = [sem(f"wm_in{i}") for i in range(2 * UNITS)]
        ident_ok = sem("ident_ok")
        small_t = sem("small_t")
        small_ok = sem("small_ok")
        cond_ok = sem("cond_ok")
        mod_mm = sem("mod_mm")
        mod_row = sem("mod_row")
        mod_t = sem("mod_t")
        mod_col = sem("mod_col")
        rel_zero = sem("rel_zero")
        rel_in = sem("rel_in")
        rel_out = sem("rel_out")
        block = ctx.enter_context(nc.Block())

        @block.sync
        def _(sp):
            for name, (a, b) in SMALL.items():
                src = {"c": io["c"], "c_ctx": io["c_ctx"].rearrange("(a d) -> a d", a=1),
                       "norm1": io["norm1"], "norm2": io["norm2"], "out_norm_a": io["out_norm_a"],
                       "out_norm_b": io["out_norm_b"], "b_s": io["b_s"][0], "b_mod": io["b_mod"]}[name]
                if name != "b_s":
                    src = src.rearrange("a (r p) -> (a r) p", p=P)
                sp.dma_start(small_rows[a:b, :], src).then_inc(small_in, 16)
            for u in range(UNITS):
                for half in range(2):
                    ks = slice(half * KD // 2, (half + 1) * KD // 2)
                    sp.dma_start(wm[:, u, ks], w_mod[u][:, ks]).then_inc(wm_in[2 * u + half], 16)

        @block.gpsimd
        def _(pool):
            ident = keep["ident"]
            pool.memset(ident[:, :], 0.0).then_inc(ident_ok, 1)
            pool.wait_ge(ident_ok, 1)
            pool.affine_select(out=ident[:, :], in_=ident[:, :], compare_op=ALU.not_equal, fill=1.0,
                               base=0, pattern=[[-1, P]], channel_multiplier=1).then_inc(ident_ok, 1)
            pool.memset(keep["minus_half"][:, :], -0.5)
            pool.memset(keep["eps"][:, :], EPS)
            pool.wait_ge(rel_zero, 1)
            at = GRID_W - WIN_W
            rpb = io["rpb"][0].rearrange("h r c -> (h r) c").partition_broadcast(GRID_W)
            pool.dma_start(rel[:, :, at:at + RPB_W], rpb).then_inc(rel_in, 16)
            pool.wait_ge(rel_in, 16)
            pool.dma_start(scratch["rel"].rearrange("r q c -> q r c"), rel[:, :, :]).then_inc(rel_out, 16)
            pool.wait_ge(rel_out, 16)

        @block.scalar
        def _(act):
            a, b = SMALL["c"][0], SMALL["c_ctx"][1]
            act.wait_ge(small_ok, 1)
            act.activation(cond[:, :, :].rearrange("p a k -> p (a k)"), keep["small"][:, a:b],
                           ACT.Silu).then_inc(cond_ok, 1)

        @block.tensor
        def _(pe):
            ident = keep["ident"]
            pe.wait_ge(ident_ok, 2)
            pe.wait_ge(small_in, 16 * len(SMALL))
            pe.transpose(ps_t[:, 0:SMALL_ROWS], small_rows[:, :],
                         ident[0:SMALL_ROWS, 0:SMALL_ROWS]).then_inc(small_t, 1)
            pe.wait_ge(cond_ok, 1)
            for u in range(UNITS):
                if u >= 2:
                    pe.wait_ge(mod_row, u - 1)
                for k in range(KD):
                    if k % (KD // 2) == 0:
                        pe.wait_ge(wm_in[2 * u + k // (KD // 2)], 16)
                    mm = pe.matmul(ps_m[u % 2][0:2, :], cond[:, :, k], wm[:, u, k, :],
                                   start=(k == 0), stop=(k == KD - 1))
                mm.then_inc(mod_mm, 1)
            pe.wait_ge(mod_row, UNITS)
            for i in range(COLS):
                t = pe.transpose(ps_t[:, 128 + 2 * i:130 + 2 * i], mod_rows[:, i * P:(i + 1) * P],
                                 ident[0:2, 0:2])
            t.then_inc(mod_t, 1)

        @block.vector
        def _(dve):
            dve.memset(rel[:, :, :], 0.0).then_inc(rel_zero, 1)
            dve.wait_ge(small_t, 1)
            dve.tensor_copy(keep["small"][:, :], ps_t[:, 0:SMALL_ROWS]).then_inc(small_ok, 1)
            for u in range(UNITS):
                cols = slice(u * BANK, (u + 1) * BANK)
                dve.wait_ge(mod_mm, u + 1)
                dve.tensor_copy(mod_rows[:, cols], ps_m[u % 2][0:2, :]).then_inc(mod_row, 1)
            dve.wait_ge(mod_t, 1)
            b_mod = keep["small"][:, SMALL["b_mod"][0]:SMALL["b_mod"][0] + COLS]
            dve.tensor_tensor(mod_cols[:, :, :], ps_t[:, 128:128 + 2 * COLS].rearrange("p (m a) -> p m a", a=2),
                              b_mod[:, :, None].broadcast_to([P, COLS, 2]), ALU.add).then_inc(mod_col, 1)
            dve.wait_ge(mod_col, 1)
            lo, hi = SMALL["norm1"]
            for a, name in enumerate("1c"):
                dve.scalar_tensor_tensor(out=keep["gain" + name][:, :], in0=mod_cols[:, KD:2 * KD, a], scalar=1.0,
                                         in1=keep["small"][:, lo:hi], op0=ALU.add, op1=ALU.mult)
                dve.tensor_copy(keep["shift" + name][:, :], mod_cols[:, 0:KD, a])


def projection_phase(nc, sem, io, scratch, keep, tag, x_rows, n_super, tiles, blocks, gain, shift, out):
    NT = tiles * P
    NB = min(BANK, NT)
    PAIRS = tiles // 2
    HALF_K = KD // 2
    GB = 4
    AHEAD = n_super > 1
    TURNS = 2 if AHEAD else 1
    NBLK = len(blocks)
    w_in = io["w_in"][0].rearrange("(j k p) n -> j p k n", p=P, k=HALF_K)
    gmlp = "z" in blocks
    col_at = {"q": 0, "k": NA, "v": 2 * NA, "u": 3 * NA, "z": 3 * NA + SG}

    groups = []
    for c, name in enumerate(blocks):
        if name in "qk":
            groups += [(c, name, i, h) for h in range(NT // NB) for i in range(KNA)]
        else:
            groups += [(c, name, i, 0) for i in range(tiles)]
        if AHEAD and c:
            groups.insert(groups.index((c, name, 0, 0)) + 1, (c, "m", 0, 0))
    first = [min(n for n, g in enumerate(groups) if g[0] == c) for c in range(len(blocks))]
    last = [max(n for n, g in enumerate(groups) if g[0] == c) for c in range(len(blocks))]
    NP, NG = 2 * PAIRS, len(groups)
    bank_uses = [len(range(b, NG, GB)) for b in range(GB)]
    SQUARE_AT, NORM_AT = {1: 0, 3: 1, 12: 2, 13: 3}, {2: 0, 4: 1, 13: 2, 14: 3}
    TURN_AT, MODULATE_AT, SPLIT_AT = ({at + lag: m for m, at in enumerate((8, 11, 17, 19))} for lag in range(3))
    SPLIT_W_AT = ((0, 1), (1, 3))
    WEIGH_AT = [first[c] + min(1 + c, 2) for c in range(NBLK - 1)]
    if not AHEAD:
        SQUARE_AT = NORM_AT = TURN_AT = MODULATE_AT = SPLIT_AT = WEIGH_AT = {}
    stores = [n for n, g in enumerate(groups) if g[1] in "qkvu"]
    POOL_LINKS = tiles * 3
    FIRST_BANKS = (0, 2)
    MOD_UNITS = (N_MOD - EARLY) * KD
    STEP_UNITS = MOD_UNITS // n_super
    DVE_LINKS = NP + tiles * 3 + STEP_UNITS * (KD - 1)

    with ExitStack() as ctx:
        def sb(name, shape, dt=F32):
            return ctx.enter_context(nc.sbuf_tensor(f"{tag}_{name}", shape, dt))

        hT_hi = [sb(f"hT_hi{i}", [P, KD, NT], F32R) for i in range(TURNS)]
        hT_lo = [sb(f"hT_lo{i}", [P, KD, NT], F32R) for i in range(TURNS)]
        w_hi = sb("w_hi", [P, 2, KD, BANK], F32R)
        w_lo = sb("w_lo", [P, 2, KD, BANK], F32R)
        w_raw = sb("w_raw", [P, 2, HALF_K, BANK])
        xin = sb("xin", [P, 2, D])
        xr = sb("xr", [P, 2, D])
        stat = sb("stat", [P, 8, 8])
        h_full = sb("h_full", [P, 2, HALF_K, 2 * P])
        stage = sb("stage", [P, 4, BANK])
        if gmlp:
            spatial = sb("spatial", [P, tiles, SG])
            act_out = sb("act_out", [P, 2, SG])
            zn = sb("zn", [P, SG])
            ws_raw = spatial[:, 0:2].rearrange("p a (g q) -> p (a g) q", q=P)
            wsT = sb("wsT", [P, GROUPS, P])
            z_gain = sb("z_gain", [P, SG])
            wm = sb("wm", [P, KD, P])
            table = sb("table", [P, SLOTS, GRID_W])
            weighted = sb("weighted", [P, 2, P])
            one = sb("one", [P, 1])
            mod_cols = sb("mod_cols", [P, MOD_UNITS])
            mod_rows = zn[0:MOD_UNITS, 0:P]
            w_mod = io["w_mod"][0].rearrange("(k p) (u n) -> u p k n", p=P, n=P)
        bank = [ctx.enter_context(nc.psum_tensor(f"{tag}_bank{i}", [P, BANK], F32)) for i in range(8)]
        x_in = [sem(f"{tag}_x_in{i}") for i in range(2)]
        x_sq = sem(f"{tag}_x_sq")
        x_norm = sem(f"{tag}_x_norm")
        x_rstd = sem(f"{tag}_x_rstd")
        z_var = sem(f"{tag}_z_var")
        passed = sem(f"{tag}_passed")
        pool_passed = sem(f"{tag}_pool_passed")
        z_rstd = sem(f"{tag}_z_rstd")
        ob_rstd = sem(f"{tag}_ob_rstd")
        xr_free = sem(f"{tag}_xr_free")
        piece_t = sem(f"{tag}_piece_t")
        piece_full = sem(f"{tag}_piece_full")
        piece_lo = sem(f"{tag}_piece_lo")
        w_loaded = [sem(f"{tag}_w_loaded{i}") for i in range(2)]
        w_hi_ok = sem(f"{tag}_w_hi_ok")
        w_split = sem(f"{tag}_w_split")
        w_free = [sem(f"{tag}_w_free{i}") for i in range(2)]
        hT_free = sem(f"{tag}_hT_free")
        bank_free = [sem(f"{tag}_bank_free{i}") for i in range(GB)]
        product = sem(f"{tag}_product")
        staged = [sem(f"{tag}_staged{i}") for i in range(4)]
        stored = [sem(f"{tag}_stored{i}") for i in range(4)]
        dve_link = sem(f"{tag}_dve_link")
        pool_link = sem(f"{tag}_pool_link")
        gelu_ok = sem(f"{tag}_gelu_ok")
        zn_ok = sem(f"{tag}_zn_ok")
        gelu_used = sem(f"{tag}_gelu_used")
        mixed = sem(f"{tag}_mixed")
        mix_free = sem(f"{tag}_mix_free")
        ob_ok = sem(f"{tag}_ob_ok")
        ob_sq = sem(f"{tag}_ob_sq")
        ws_in = sem(f"{tag}_ws_in")
        ws_t = sem(f"{tag}_ws_t")
        ws_ok = sem(f"{tag}_ws_ok")
        wm_in = sem(f"{tag}_wm_in")
        wm_used = sem(f"{tag}_wm_used")
        weight_ok = sem(f"{tag}_weight_ok")
        mod_ok = sem(f"{tag}_mod_ok")
        mod_end = sem(f"{tag}_mod_end")
        mod_t = sem(f"{tag}_mod_t")
        mod_row = sem(f"{tag}_mod_row")
        mod_out = sem(f"{tag}_mod_out")
        table_set = sem(f"{tag}_table_set")
        table_in = sem(f"{tag}_table_in")
        table_cut = sem(f"{tag}_table_cut")
        table_out = sem(f"{tag}_table_out")
        block = ctx.enter_context(nc.Block())

        def w_use(i, g):
            return i * TURNS * NBLK + g, g % 2, i * (TURNS * NBLK // 2) + g // 2

        @block.sync
        def _(sp):
            if gmlp:
                sp.dma_start(ws_raw[:, :, :], io["w_s"][0].rearrange("g p q -> p g q")).then_inc(ws_in, 16)
                sp.dma_start(z_gain[:, :], io["gmlp_norm"].rearrange("a d -> (a d)").partition_broadcast(P)
                             ).then_inc(ws_in, 16)

            def load_w(i, g):
                n, _, _ = w_use(i, g)
                a = col_at[blocks[g % NBLK]]
                for j in range(2):
                    sp.wait_ge(w_split, n * 2 + j + 1)
                    sp.dma_start(w_raw[:, j], w_in[j, :, :, a:a + BANK]).then_inc(w_loaded[j], 16)

            def load_unit(s, c, j):
                unit = s * STEP_UNITS + c * 2 + j
                sp.wait_ge(wm_used, unit + 1)
                sp.dma_start(wm[:, :, :], w_mod[EARLY * KD + unit % MOD_UNITS]).then_inc(wm_in, 16)

            def load_x(s, t, src):
                sp.wait_ge(x_norm, s * tiles + t + 1)
                sp.dma_start(xin[:, t % 2], src).then_inc(x_in[t % 2], 16)
            for t in range(tiles):
                load_x(0, t, x_rows[0, t])
                if t == 1:
                    load_w(0, 0)
            load_w(0, 1)
            if AHEAD:
                load_unit(0, 0, 0)
            with each(sp, n_super // TURNS) as i:
                for par in range(TURNS):
                    s = i * TURNS + par
                    for c in range(NBLK):
                        if AHEAD and c < 2:
                            for t in (2 * c, 2 * c + 1):
                                load_x(s + 1, t, x_rows[(s + 1) % n_super, t])
                        for n in range(first[c], last[c] + 1):
                            _, name, a, h = groups[n]
                            if n in stores:
                                k = stores.index(n)
                                slot = k % 4
                                sp.wait_ge(staged[slot], s * (len(stores) // 4) + k // 4 + 1)
                                dst = (out[name][s, a, :, h * NB:(h + 1) * NB] if name in "qk"
                                       else out[name][s, a])
                                sp.dma_start(dst, stage[:, slot, 0:dst.shape[-1]]).then_inc(stored[slot], 16)
                            if n in WEIGH_AT:
                                load_unit(s, c, 1)
                            if AHEAD and n == first[c] + 1:
                                load_w(i, par * NBLK + c + 2)
                            if AHEAD and n == last[c] and c + 1 < NBLK:
                                load_unit(s, c + 1, 0)
            if AHEAD:
                for loaded in w_loaded:
                    sp.wait_ge(loaded, (n_super * NBLK + 2) * 16)
                sp.wait_ge(wm_in, (MOD_UNITS + 1) * 16)
                sp.wait_ge(mod_row, 1)
                sp.dma_start(scratch["mod"].rearrange("(u n) -> u n", n=P), mod_rows).then_inc(mod_out, 16)
                sp.wait_ge(mod_out, 16)
            for slot in range(4):
                sp.wait_ge(stored[slot], 16 + 16 * n_super * len(stores[slot::4]))

        @block.gpsimd
        def _(pool):
            def rstd(dst, src, n):
                pool.tensor_tensor(dst, src, keep["eps"][:, :], ALU.add).then_inc(pool_link, 1)
                pool.wait_ge(pool_link, n)
                return pool.tensor_tensor(dst, dst, keep["minus_half"][:, :], ALU.pow)

            def load_bias(head):
                if head is not None:
                    pool.wait_ge(table_out, head * 16)
                skewed = bass.AP(scratch["rel"].tensor, GRID_W - 1,
                                 [[RPB_H * GRID_W * 2 * GRID_W, HEADS], [2 * GRID_W - 1, GRID_W],
                                  [GRID_W * 2 * GRID_W, RPB_H], [1, GRID_W]])[0 if head is None else head % HEADS]
                for rr in range(2):
                    pool.dma_start(table[rr * GRID_W:(rr + 1) * GRID_W, rr:rr + RPB_H, :], skewed
                                   ).then_inc(table_in, 16)

            def store_bias(head):
                pool.wait_ge(table_in, (head + 1) * 32)
                n = head * 4
                apart(pool, pool_passed)
                for rr in range(2):
                    half = table[rr * GRID_W:(rr + 1) * GRID_W]
                    low, high = half[:, :, 0:GRID_W - WIN_W], half[:, :, WIN_W:GRID_W]
                    for cols, base, sign in ((low, WIN_W // 2, 1), (high, WIN_W // 2 - 1 - WIN_W, -1)):
                        pool.affine_select(out=cols, in_=cols, compare_op=ALU.is_ge, fill=MASKED, base=base,
                                           pattern=[[0, SLOTS], [sign, GRID_W - WIN_W]],
                                           channel_multiplier=-sign).then_inc(table_cut, 1)
                        n = n + 1
                        pool.wait_ge(table_cut, n)
                        apart(pool, pool_passed)
                pool.dma_start(scratch["table"][:, head], table[:, :, :]).then_inc(table_out, 16)

            def token_rstd(s, t, n):
                pool.wait_ge(x_sq, s * tiles + t + 1)
                rstd(stat[:, 1, t:t + 1], stat[:, 0, t:t + 1], n).then_inc(x_rstd, 1)
            if gmlp:
                pool.memset(table[:, :, :], MASKED).then_inc(table_set, 1)
                pool.wait_ge(table_set, 1)
            for t in range(tiles):
                token_rstd(0, t, t + 1)
            if gmlp:
                load_bias(None)
                with each(pool, n_super) as s:
                    done = s * POOL_LINKS + tiles
                    for t in range(tiles):
                        token_rstd(s + 1, t, done + t + 1)
                        if t == 0:
                            store_bias(s * 2)
                        if t == 2:
                            load_bias(s * 2 + 1)
                    for a in range(tiles):
                        pool.wait_ge(z_var, s * tiles + a + 1)
                        rstd(stat[:, 3, 2:3], stat[:, 3, 1:2], done + tiles + a + 1).then_inc(z_rstd, 1)
                    for a in range(tiles):
                        pool.wait_ge(ob_sq, s * tiles + a + 1)
                        rstd(stat[:, 6, a:a + 1], stat[:, 4, a:a + 1], done + 2 * tiles + a + 1
                             ).then_inc(ob_rstd, 1)
                        if a == 0:
                            store_bias(s * 2 + 1)
                    load_bias(s * 2 + 2)
                pool.wait_ge(table_in, (HEADS + 1) * 32)
                pool.wait_ge(table_out, HEADS * 16)

        def stage_slot(eng, s, n):
            i = stores.index(n)
            eng.wait_ge(stored[i % 4], (s * (len(stores) // 4) + i // 4 + 1) * 16)
            return i % 4

        @block.scalar
        def _(act):
            def split(i, g, j):
                n, slot, before = w_use(i, g)
                act.wait_ge(w_loaded[j], (n + 1) * 16)
                act.wait_ge(w_free[slot], before + 1)
                act.activation(w_hi[:, slot, j * HALF_K:(j + 1) * HALF_K, :], w_raw[:, j],
                               ACT.Copy).then_inc(w_hi_ok, 1)

            def square(s, t):
                act.wait_ge(x_in[t % 2], (s * PAIRS + t // 2 + 1) * 16)
                act.wait_ge(xr_free, s * tiles + t + 1)
                act.activation(xr[:, t % 2], xin[:, t % 2], ACT.Square, scale=float(D) ** -0.5,
                               accum_out=stat[:, 0, t:t + 1]).then_inc(x_sq, 1)

            def modulate(s, m, at=4):
                act.wait_ge(piece_t, s * NP + m + 1)
                act.wait_ge(piece_lo, s * NP + m + 1)
                for i in range(HALF_K):
                    k = (m % 2) * HALF_K + i
                    act.activation(h_full[:, m % 2, i], bank[at + i // 2][:, (i % 2) * 256:(i % 2) * 256 + 256],
                                   ACT.Identity, scale=gain[:, k:k + 1], bias=shift[:, k:k + 1]
                                   ).then_inc(piece_full, 1)
            square(0, 0)
            square(0, 1)
            split(0, 0, 0)
            split(0, 0, 1)
            for m in range(NP):
                modulate(0, m, FIRST_BANKS[m % 2])
                if m % 2 == 0 and m + 2 < NP:
                    square(0, m + 2)
                    square(0, m + 3)
            with each(act, n_super // TURNS) as i:
                for par in range(TURNS):
                    s = i * TURNS + par
                    for n, (c, name, a, h) in enumerate(groups):
                        halves_at = SPLIT_W_AT[blocks[c] == "z"]
                        if name in "quz":
                            act.wait_ge(product, s * NG + n + 1)
                            b = n % GB
                            if name == "q":
                                slot = stage_slot(act, s, n)
                                act.activation(stage[:, slot, 0:NB], bank[b][:, 0:NB], ACT.Copy,
                                               scale=float(DH) ** -0.5).then_inc(staged[slot], 1)
                                act.wait_ge(staged[slot], s * (len(stores) // 4) + stores.index(n) // 4 + 1)
                                act.sem_inc(bank_free[b], 1)
                            else:
                                m = [g for g in range(len(groups)) if groups[g][1] in "uz"].index(n)
                                act.wait_ge(gelu_used, s * 2 * tiles + m + 1)
                                act.activation(act_out[:, m % 2], bank[b][:, :], ACT.Gelu_apprx_tanh
                                               ).then_inc(gelu_ok, 1)
                                act.wait_ge(gelu_ok, s * 2 * tiles + m + 1)
                                act.sem_inc(bank_free[b], 1)
                            if name == "u":
                                act.wait_ge(ob_ok, s * tiles + a + 1)
                                act.activation(zn[:, :], spatial[:, a], ACT.Square,
                                               scale=float(SG) ** -0.5,
                                               accum_out=stat[:, 4, a:a + 1]).then_inc(ob_sq, 1)
                        if (AHEAD or c + 1 < NBLK) and n - first[c] in halves_at:
                            split(i, par * NBLK + c + 1, halves_at.index(n - first[c]))
                        if n in SQUARE_AT:
                            square(s + 1, SQUARE_AT[n])
                        if n in MODULATE_AT:
                            modulate(s + 1, MODULATE_AT[n])

        @block.vector
        def _(dve):
            dve.sem_inc(x_norm, 2)
            dve.sem_inc(xr_free, 2)
            dve.sem_inc(piece_lo, 2)
            dve.sem_inc(w_split, 2)
            dve.sem_inc(hT_free, 2)
            dve.sem_inc(piece_full, HALF_K)
            for slot in range(4):
                dve.sem_inc(stored[slot], 16)
            dve.sem_inc(w_free[0], 1)
            dve.sem_inc(w_free[1], 1)
            for b in range(GB):
                dve.sem_inc(bank_free[b], 1)
            if gmlp:
                dve.sem_inc(gelu_used, 2)
                dve.sem_inc(mix_free, 2)
                for g in range(2):
                    dve.wait_ge(ws_t, g + 1)
                    dve.tensor_copy(wsT[:, 4 * g:4 * g + 4, :].rearrange("p g q -> p (g q)"),
                                    bank[6 + g][:, :]).then_inc(ws_ok, 1)
                dve.wait_ge(ws_in, 32)
                dve.sem_inc(wm_used, 1)
                dve.sem_inc(mod_ok, 1)
                dve.memset(one[:, :], 1.0)

            def split(i, g, j):
                n, slot, _ = w_use(i, g)
                dve.wait_ge(w_hi_ok, n * 2 + j + 1)
                half = slice(j * HALF_K, (j + 1) * HALF_K)
                dve.tensor_tensor(w_lo[:, slot, half, :], w_raw[:, j], w_hi[:, slot, half, :].bitcast(F32),
                                  ALU.subtract).then_inc(w_split, 1)

            def normalise(s, t):
                dve.wait_ge(x_rstd, s * tiles + t + 1)
                dve.tensor_scalar(xr[:, t % 2], xin[:, t % 2], stat[:, 1, t:t + 1], None,
                                  ALU.mult).then_inc(x_norm, 1)

            def split_piece(s, par, m, link):
                dve.wait_ge(piece_full, (s * NP + m + 2) * HALF_K)
                if m == 0:
                    dve.wait_ge(hT_free, s + 1)
                ks = slice((m % 2) * HALF_K, (m % 2 + 1) * HALF_K)
                cols = slice(m // 2 * 2 * P, (m // 2 + 1) * 2 * P)
                hi, lo = hT_hi[par][:, ks, cols], hT_lo[par][:, ks, cols]
                link(dve.tensor_copy(hi, h_full[:, m % 2]))
                dve.tensor_tensor(lo, h_full[:, m % 2], hi.bitcast(F32), ALU.subtract).then_inc(piece_lo, 1)

            def weight(s, c, j, link):
                unit = s * STEP_UNITS + c * 2 + j
                dve.wait_ge(wm_in, (unit + 1) * 16)
                acc = weighted[:, j, :]
                for k in range(KD):
                    c_k = keep["cond"][:, 0, k:k + 1]
                    if k == 0:
                        link(dve.tensor_scalar(acc, wm[:, k], c_k, None, ALU.mult))
                    elif k + 1 < KD:
                        link(dve.scalar_tensor_tensor(out=acc, in0=wm[:, k], scalar=c_k, in1=acc,
                                                      op0=ALU.mult, op1=ALU.add))
                    else:
                        dve.scalar_tensor_tensor(out=acc, in0=wm[:, k], scalar=c_k, in1=acc,
                                                 op0=ALU.mult, op1=ALU.add).then_inc(weight_ok, 1)
                dve.wait_ge(weight_ok, unit + 1)
                dve.sem_inc(wm_used, 1)
            normalise(0, 0)
            normalise(0, 1)
            split(0, 0, 0)
            split(0, 0, 1)
            first_link = Chain(dve, dve_link)
            for m in range(NP):
                split_piece(0, 0, m, first_link)
                if m % 2 == 0 and m + 2 < NP:
                    normalise(0, m + 2)
                    normalise(0, m + 3)
            with each(dve, n_super // TURNS) as i:
                for par in range(TURNS):
                    s = i * TURNS + par
                    link = Chain(dve, dve_link, NP + s * DVE_LINKS)

                    def spatial_out(a):
                        dve.wait_ge(mixed, s * tiles + a + 2)
                        dve.tensor_tensor(
                            spatial[:, a].rearrange("p (g d) -> p g d", g=GROUPS),
                            bank[6 + a % 2][:, :].rearrange("p (g d) -> p g d", g=GROUPS),
                            keep["small"][:, SMALL["b_s"][0]:SMALL["b_s"][1], None].broadcast_to([P, GROUPS, GD]),
                            ALU.add).then_inc(mix_free, 1)
                    for n, (c, name, a, h) in enumerate(groups):
                        halves_at = SPLIT_W_AT[blocks[c] == "z"]
                        b = n % GB
                        if name in "kv":
                            dve.wait_ge(product, s * NG + n + 1)
                            slot = stage_slot(dve, s, n)
                            w = NB if name == "k" else BANK
                            dve.tensor_copy(stage[:, slot, 0:w], bank[b][:, 0:w]).then_inc(staged[slot], 1)
                            dve.wait_ge(staged[slot], s * (len(stores) // 4) + stores.index(n) // 4 + 1)
                            dve.sem_inc(bank_free[b], 1)
                        if name == "m":
                            dve.wait_ge(product, s * NG + n + 1)
                            at = s * STEP_UNITS + (c - 1) * 2
                            dve.tensor_copy(mod_cols[:, bass.ds(at, 2)], bank[b][:, 0:2]).then_inc(mod_ok, 1)
                            dve.wait_ge(mod_ok, s * (STEP_UNITS // 2) + c + 1)
                            dve.sem_inc(bank_free[b], 1)
                        if name == "z":
                            dve.wait_ge(gelu_ok, s * 2 * tiles + a + 1)
                            z = act_out[:, a % 2]
                            link(dve.bn_stats(stat[:, 2, 0:6], z))
                            apart(dve, passed)
                            dve.bn_aggr(stat[:, 3, 0:2], stat[:, 2, 0:6]).then_inc(z_var, 1)
                            if a >= 1:
                                spatial_out(a - 1)
                            dve.wait_ge(z_rstd, s * tiles + a + 1)
                            link(dve.tensor_scalar(zn[:, :], z, stat[:, 3, 0:1], stat[:, 3, 2:3],
                                                   ALU.subtract, ALU.mult))
                            dve.sem_inc(gelu_used, 1)
                            dve.tensor_tensor(zn[:, :], zn[:, :], z_gain[:, :], ALU.mult).then_inc(zn_ok, 1)
                        if name == "u":
                            if a == 0:
                                spatial_out(tiles - 1)
                            dve.wait_ge(gelu_ok, s * 2 * tiles + tiles + a + 1)
                            dve.wait_ge(mix_free, s * tiles + tiles + 2)
                            dve.tensor_tensor(spatial[:, a], spatial[:, a], act_out[:, a % 2],
                                              ALU.mult).then_inc(ob_ok, 1)
                            dve.wait_ge(ob_ok, s * tiles + a + 1)
                            dve.sem_inc(gelu_used, 1)
                            dve.wait_ge(ob_rstd, s * tiles + a + 1)
                            slot = stage_slot(dve, s, n)
                            link(dve.tensor_scalar(stage[:, slot, :], spatial[:, a], stat[:, 6, a:a + 1], None,
                                                   ALU.mult))
                            dve.sem_inc(staged[slot], 1)
                        if (AHEAD or c + 1 < NBLK) and n - first[c] in halves_at:
                            split(i, par * NBLK + c + 1, halves_at.index(n - first[c]))
                        if n in WEIGH_AT:
                            dve.wait_ge(mod_ok, s * (STEP_UNITS // 2) + c + 1)
                            weight(s, c, 0, link)
                        if AHEAD and c + 1 < NBLK and n == last[c]:
                            weight(s, c, 1, link)
                        if n in NORM_AT:
                            normalise(s + 1, NORM_AT[n])
                        if n in SPLIT_AT:
                            split_piece(s + 1, 1 - par, SPLIT_AT[n], link)
                    assert not AHEAD or link.n == DVE_LINKS, (link.n, DVE_LINKS)
            if AHEAD:
                a, b = SMALL["b_mod"]
                dve.wait_ge(mod_ok, MOD_UNITS // 2 + 1)
                dve.tensor_tensor(mod_cols[:, :], mod_cols[:, :], keep["small"][:, a + EARLY * KD:b],
                                  ALU.add).then_inc(mod_end, 1)
                dve.wait_ge(mod_end, 1)
                lo, hi = SMALL["norm2"]
                dve.scalar_tensor_tensor(out=keep["gain2"][:, :], in0=mod_cols[:, 2 * KD:3 * KD], scalar=1.0,
                                         in1=keep["small"][:, lo:hi], op0=ALU.add, op1=ALU.mult)
                dve.tensor_copy(keep["shift2"][:, :], mod_cols[:, KD:2 * KD])
                dve.wait_ge(mod_t, 1)
                dve.tensor_copy(mod_rows, bank[0][0:MOD_UNITS, 0:P]).then_inc(mod_row, 1)

        @block.tensor
        def _(pe):
            if gmlp:
                pe.sem_inc(mixed, 1)
                pe.wait_ge(ws_in, 32)
                for g in range(GROUPS):
                    t = pe.transpose(bank[6 + g // 4][:, (g % 4) * P:(g % 4 + 1) * P], ws_raw[:, g, :],
                                     keep["ident"][:, :])
                    if g % 4 == 3:
                        t.then_inc(ws_t, 1)
                pe.wait_ge(ws_ok, 2)

            def turn(s, m, at=4):
                if m % 2 == 0:
                    pe.wait_ge(x_norm, s * tiles + m + 4)
                if at == 4:
                    pe.wait_ge(piece_full, (s * NP + m + 1) * HALF_K)
                elif m >= 2:
                    pe.wait_ge(piece_full, m * HALF_K)
                for i in range(HALF_K):
                    k = (m % 2) * HALF_K + i
                    for j in range(2):
                        a = (i % 2) * 256 + j * P
                        t = pe.transpose(bank[at + i // 2][:, a:a + P], xr[:, j, k * P:(k + 1) * P],
                                         keep["ident"][:, :])
                t.then_inc(piece_t, 1)
                if m % 2:
                    pe.wait_ge(piece_t, s * NP + m + 1)
                    pe.sem_inc(xr_free, 2)
            for m in range(NP):
                turn(0, m, FIRST_BANKS[m % 2])
            with each(pe, n_super // TURNS) as i:
                for par in range(TURNS):
                    s = i * TURNS + par

                    def mix(a):
                        pe.wait_ge(zn_ok, s * tiles + a + 1)
                        pe.wait_ge(mix_free, s * tiles + a + 1)
                        for g in range(GROUPS):
                            mm = pe.matmul(bank[6 + a % 2][:, g * GD:(g + 1) * GD], wsT[:, g, :],
                                           zn[:, g * GD:(g + 1) * GD], start=True, stop=True)
                        mm.then_inc(mixed, 1)

                    pe.wait_ge(piece_lo, (s + 1) * NP + 2)
                    for n, (c, name, a, h) in enumerate(groups):
                        block_no, slot, _ = w_use(i, par * NBLK + c)
                        if n == first[c]:
                            pe.wait_ge(w_split, block_no * 2 + 4)
                        b = n % GB
                        pe.wait_ge(bank_free[b], s * bank_uses[b] + n // GB + 1)
                        wh, wl = w_hi[:, slot], w_lo[:, slot]
                        if name == "m":
                            pe.wait_ge(weight_ok, s * STEP_UNITS + c * 2)
                            for j in range(2):
                                mm = pe.matmul(bank[b][:, j:j + 1], weighted[:, j, :], one[:, :],
                                               start=True, stop=True)
                        for k in range(KD if name != "m" else 0):
                            for x, (hp, wp) in enumerate(((hT_hi[par], wh), (hT_lo[par], wh), (hT_hi[par], wl))):
                                if name in "qk":
                                    mm = pe.matmul(bank[b][:, 0:NB], wp[:, k, a * P:(a + 1) * P],
                                                   hp[:, k, h * NB:(h + 1) * NB],
                                                   start=(k == 0 and x == 0), stop=(k == KD - 1 and x == 2))
                                else:
                                    mm = pe.matmul(bank[b][:, :], hp[:, k, a * P:(a + 1) * P], wp[:, k, :],
                                                   start=(k == 0 and x == 0), stop=(k == KD - 1 and x == 2))
                        mm.then_inc(product, 1)
                        if name == "z" and a >= 1:
                            mix(a - 1)
                        if name == "u" and a == 0:
                            mix(tiles - 1)
                        if n == last[c]:
                            pe.wait_ge(product, s * NG + n + 1)
                            pe.sem_inc(w_free[slot], 1)
                        if n in TURN_AT:
                            turn(s + 1, TURN_AT[n])
                    pe.sem_inc(hT_free, 1)
            if AHEAD:
                pe.wait_ge(mod_end, 1)
                pe.wait_ge(bank_free[0], n_super * bank_uses[0] + 1)
                pe.transpose(bank[0][0:MOD_UNITS, 0:P], mod_cols[:, :], keep["ident"][:, :]).then_inc(mod_t, 1)

def attention_phase(nc, sem, io, scratch, keep):
    PIECES = 4
    KP, QP = (SEQ + CTX) // PIECES, SEQ // PIECES
    INTERIOR = EDGE
    LAG_EXP, LAG_T, LAG_PV, LAG_O = 1, 2, 3, 4

    def local_rows(j):
        if j < EDGE:
            return 0, WIN_H
        if j >= BLOCKS - EDGE:
            return ROWS - WIN_H, WIN_H
        return 2 * j - WIN_H // 2, KEY_ROWS

    VARIANTS = [INTERIOR] + list(range(EDGE)) + list(range(BLOCKS - EDGE, BLOCKS))

    def variant(j):
        return VARIANTS.index(j) if j in VARIANTS else 0

    with ExitStack() as ctx:
        def sb(name, shape, dt=F32):
            return ctx.enter_context(nc.sbuf_tensor(f"att_{name}", shape, dt))

        k_raw = sb("k_raw", [P, SEQ + CTX])
        q_raw = sb("q_raw", [P, SEQ])
        k_hi = sb("k_hi", [P, 2, SEQ + CTX], F32R)
        k_lo = sb("k_lo", [P, 2, SEQ + CTX], F32R)
        q_parts = sb("q_parts", [P, 2, SEQ], F32R)
        v_sb = sb("v", [P, 2, TILES + CTX // P, DH])
        bias = sb("bias", [P, 2, len(VARIANTS), KEYS])
        neg_s = sb("neg_s", [P, 3, KEYS])
        probs = sb("probs", [P, 3, KEYS])
        probsT = sb("probsT", [P, 2, 7, P])
        low = sb("low", [P, 4])
        total = sb("total", [P, 4])
        inv = sb("inv", [P, 4])
        ps_s = [ctx.enter_context(nc.psum_tensor(f"ps_s{i}", [P, 2 * BANK], F32)) for i in range(2)]
        ps_ta = ctx.enter_context(nc.psum_tensor("ps_ta", [P, BANK], F32))
        ps_tb = ctx.enter_context(nc.psum_tensor("ps_tb", [P, BANK], F32))
        ps_o = [ctx.enter_context(nc.psum_tensor(f"ps_o{i}", [P, BANK], F32)) for i in range(2)]

        k_in = sem("att_k_in")
        q_in = sem("att_q_in")
        v_in = [sem(f"att_v_in{i}") for i in range(2)]
        bias_in = [sem(f"att_bias_in{i}") for i in range(2)]
        bias_ok = sem("att_bias_ok")
        rounded = sem("att_rounded")
        split_ok = sem("att_split_ok")
        scored = sem("att_scored")
        biased = sem("att_biased")
        exped = sem("att_exped")
        turned = sem("att_turned")
        turned_a = sem("att_turned_a")
        turned_b = sem("att_turned_b")
        summed = sem("att_summed")
        inverted = sem("att_inverted")
        w_out_in = sem("att_w_out_in")
        pool_passed = sem("att_pool_passed")
        dve_passed = sem("att_dve_passed")
        sp_passed = sem("att_sp_passed")
        output = sem("att_output")
        block = ctx.enter_context(nc.Block())
        kT, kTc = scratch["kT"], scratch["kTc"]
        qT = scratch["qT"]
        v_rows = scratch["v"].rearrange("(t p) n -> p t n", p=P)
        vc_rows = scratch["vc"].rearrange("(t p) n -> p t n", p=P)

        @block.sync
        def _(sp):
            def load(head, done, par):
                rows = bass.ds(head * DH, DH)
                if done is not None:
                    sp.wait_ge(split_ok, (done + 1) * 2 * PIECES)
                for half in range(2):
                    part = slice(half * DH, (half + 1) * DH)
                    sp.dma_start(k_raw[part, 0:SEQ], kT[rows, :]).then_inc(k_in, 16)
                    sp.dma_start(k_raw[part, SEQ:SEQ + CTX], kTc[rows, :]).then_inc(k_in, 16)
                    sp.dma_start(q_raw[part, :], qT[rows, :]).then_inc(q_in, 16)
                if done is not None:
                    sp.wait_ge(summed, done * BLOCKS + 2)
                    apart(sp, sp_passed)
                cols = bass.ds(head * DH, DH)
                sp.dma_start(v_sb[:, par, 0:TILES, :], v_rows[:, :, cols]).then_inc(v_in[par], 16)
                sp.dma_start(v_sb[:, par, TILES:, :], vc_rows[:, :, cols]).then_inc(v_in[par], 16)
                if done is not None:
                    sp.wait_ge(biased, done * BLOCKS + 2)
                for v, j in enumerate(VARIANTS):
                    base, rows_n = local_rows(j)
                    slot = base - 2 * j + WIN_H - 1
                    src = scratch["table"].rearrange("p h m k -> h p (m k)")[head]
                    sp.dma_start(bias[:, par, v, 0:rows_n * GRID_W],
                                 src[:, slot * GRID_W:(slot + rows_n) * GRID_W]).then_inc(bias_in[par], 16)
            load(0, None, 0)
            with sp.Fori(0, HEADS // 2) as i:
                for par in range(2):
                    load((i * 2 + par + 1) % HEADS, i * 2 + par, 1 - par)
            sp.wait_ge(v_in[0], 32 * (HEADS // 2 + 1))

        BIAS_OK0 = 2 * len(VARIANTS)

        @block.gpsimd
        def _(pool):
            for par in range(2):
                for v, j in enumerate(VARIANTS):
                    n = local_rows(j)[1] * GRID_W
                    pool.memset(bias[:, par, v, n:n + CTX], 0.0).then_inc(bias_ok, 1)

            def mask(par, n, nth):
                pool.wait_ge(bias_in[par], 16 * len(VARIANTS) * nth)
                pool.wait_ge(bias_ok, BIAS_OK0 + 2 * n - 2)
                apart(pool, pool_passed)
                pool.memset(bias[0:GRID_W, par, 0, WIN_H * GRID_W:LOCAL], MASKED).then_inc(bias_ok, 1)
                pool.wait_ge(bias_ok, BIAS_OK0 + 2 * n - 1)
                apart(pool, pool_passed)
                pool.memset(bias[GRID_W:P, par, 0, 0:GRID_W], MASKED).then_inc(bias_ok, 1)
            mask(0, 1, 1)
            pool.dma_start(keep["w_out"][:, :, :], io["w_out"][0].rearrange("(k p) n -> p k n", p=P)
                           ).then_inc(w_out_in, 16)
            with pool.Fori(0, HEADS // 2) as i:
                for par in range(2):
                    mask(1 - par, i * 2 + par + 2, i + 1 + par)
            pool.wait_ge(w_out_in, 16)

        @block.scalar
        def _(act):
            def split(par, head, p):
                if p < PIECES:
                    act.wait_ge(k_in, (head + 1) * 64)
                    act.activation(k_hi[:, par, p * KP:(p + 1) * KP], k_raw[:, p * KP:(p + 1) * KP],
                                   ACT.Copy).then_inc(rounded, 1)
                else:
                    p -= PIECES
                    act.wait_ge(q_in, (head + 1) * 32)
                    act.activation(q_parts[:, par, p * QP:(p + 1) * QP], q_raw[:, p * QP:(p + 1) * QP],
                                   ACT.Copy).then_inc(rounded, 1)
            for p in range(2 * PIECES):
                split(0, 0, p)
            with act.Fori(0, HEADS // 2) as i:
                for n in range(2 * BLOCKS + LAG_O):
                    par, j = n // BLOCKS, n % BLOCKS
                    if 2 <= j < 2 + 2 * PIECES and n < 2 * BLOCKS:
                        split(1 - par, i * 2 + par + 1, j - 2)
                    m = n - LAG_EXP
                    if 0 <= m < 2 * BLOCKS:
                        w = local_rows(m % BLOCKS)[1] * GRID_W + CTX
                        act.wait_ge(biased, i * 2 * BLOCKS + m + 3)
                        act.wait_ge(turned, i * 2 * BLOCKS + m + 1)
                        act.activation(probs[:, m % 3, 0:w], neg_s[:, m % 3, 0:w], ACT.Exp, scale=-1.0,
                                       bias=low[:, m % 4:m % 4 + 1],
                                       accum_out=total[:, m % 4:m % 4 + 1]).then_inc(exped, 1)
                    m = n - LAG_T
                    if 0 <= m < 2 * BLOCKS:
                        act.wait_ge(turned, i * 2 * BLOCKS + m + 4)
                        act.wait_ge(summed, i * 2 * BLOCKS + m + 1)
                        act.activation(probsT[:, m % 2, 0:4, :].rearrange("p c q -> p (c q)"), ps_ta[:, :],
                                       ACT.Copy).then_inc(turned_a, 1)

        @block.vector
        def _(dve):
            def split(par, head, p):
                dve.wait_ge(rounded, head * 2 * PIECES + p + 1)
                if p < PIECES:
                    cols = slice(p * KP, (p + 1) * KP)
                    dve.tensor_tensor(k_lo[:, par, cols], k_raw[:, cols], k_hi[:, par, cols].bitcast(F32),
                                      ALU.subtract).then_inc(split_ok, 1)
                else:
                    cols = slice((p - PIECES) * QP, (p - PIECES + 1) * QP)
                    low_half = q_parts[DH:P, par, cols]
                    dve.tensor_tensor(low_half, q_raw[DH:P, cols], low_half.bitcast(F32),
                                      ALU.subtract).then_inc(split_ok, 1)
            for s, v in ((biased, 2), (exped, 3), (turned, 3), (turned_a, 1), (turned_b, 1), (summed, 2),
                         (output, 2)):
                dve.sem_inc(s, v)
            for p in range(2 * PIECES):
                split(0, 0, p)
            with dve.Fori(0, HEADS // 2) as i:
                at = i * 2 * BLOCKS
                for n in range(2 * BLOCKS + LAG_O):
                    par, j = n // BLOCKS, n % BLOCKS
                    if n < 2 * BLOCKS:
                        w = local_rows(j)[1] * GRID_W + CTX
                        if j == 0:
                            dve.wait_ge(bias_ok, BIAS_OK0 + (i * 2 + par + 1) * 2)
                        dve.wait_ge(scored, at + n + 1)
                        dve.wait_ge(exped, at + n + 1)
                        apart(dve, dve_passed)
                        dve.tensor_tensor_reduce(neg_s[:, n % 3, 0:w], ps_s[n % 2][:, 2 * BANK - w:],
                                                 bias[:, par, variant(j), 0:w], -1.0, -MASKED, ALU.add,
                                                 ALU.min, low[:, n % 4:n % 4 + 1]).then_inc(biased, 1)
                        if 2 <= j < 2 + 2 * PIECES:
                            split(1 - par, i * 2 + par + 1, j - 2)
                    m = n - LAG_T
                    if 0 <= m < 2 * BLOCKS:
                        inner = local_rows(m % BLOCKS)[1] > WIN_H
                        a = 4 if inner else 5
                        dve.wait_ge(turned, at + m + 4)
                        dve.wait_ge(summed, at + m + 1)
                        dve.tensor_copy(probsT[:, m % 2, a:, :].rearrange("p c q -> p (c q)"),
                                        ps_tb[:, (a - 4) * P:3 * P]).then_inc(turned_b, 1)
                        dve.reciprocal(inv[:, m % 4:m % 4 + 1], total[:, m % 4:m % 4 + 1]).then_inc(inverted, 1)
                    m = n - LAG_O
                    if 0 <= m < 2 * BLOCKS:
                        dve.wait_ge(summed, at + m + 3)
                        dve.wait_ge(inverted, at + m + 1)
                        dve.tensor_scalar(
                            keep["o_a"][:, m % BLOCKS, bass.ds((i * 2 + m // BLOCKS) * DH, DH)],
                            ps_o[m % 2][:, 0:DH], inv[:, m % 4:m % 4 + 1], None, ALU.mult).then_inc(output, 1)

        @block.tensor
        def _(pe):
            with pe.Fori(0, HEADS // 2) as i:
                at = i * 2 * BLOCKS
                for n in range(2 * BLOCKS + LAG_PV):
                    if n < 2 * BLOCKS:
                        par, j = n // BLOCKS, n % BLOCKS
                        base, rows = local_rows(j)
                        if j == 0:
                            pe.wait_ge(split_ok, (i * 2 + par + 1) * 2 * PIECES)
                        pe.wait_ge(biased, at + n + 1)
                        k0 = base * GRID_W
                        first = (rows - 4) * GRID_W
                        for dst, src, width in ((BANK - first, k0, first), (BANK, k0 + first, CTX),
                                                (BANK + CTX, SEQ, CTX)):
                            for x, part in enumerate((k_hi, k_lo)):
                                mm = pe.matmul(ps_s[n % 2][:, dst:dst + width],
                                               q_parts[:, par, j * P:(j + 1) * P],
                                               part[:, par, src:src + width], start=(x == 0), stop=(x == 1))
                        mm.then_inc(scored, 1)
                    m = n - LAG_T
                    if 0 <= m < 2 * BLOCKS:
                        rows = local_rows(m % BLOCKS)[1]
                        local = rows * GRID_W
                        pe.wait_ge(exped, at + m + 4)
                        pe.wait_ge(turned_a, at + m + 1)
                        pe.wait_ge(turned_b, at + m + 1)
                        for c in range(4):
                            pe.transpose(ps_ta[:, c * P:(c + 1) * P], probs[:, m % 3, c * P:(c + 1) * P],
                                         keep["ident"][:, :])
                        if rows > WIN_H:
                            pe.transpose(ps_tb[:, 0:P], probs[:, m % 3, 4 * P:5 * P], keep["ident"][:, :])
                        for c in range(2):
                            t = pe.transpose(ps_tb[:, (c + 1) * P:(c + 2) * P],
                                             probs[:, m % 3, local + c * P:local + (c + 1) * P],
                                             keep["ident"][:, :])
                        t.then_inc(turned, 1)
                    m = n - LAG_PV
                    if 0 <= m < 2 * BLOCKS:
                        par, j = m // BLOCKS, m % BLOCKS
                        base, rows = local_rows(j)
                        if j == 0:
                            pe.wait_ge(v_in[par], (i + 1) * 32)
                        pe.wait_ge(turned_a, at + m + 2)
                        pe.wait_ge(turned_b, at + m + 2)
                        pe.wait_ge(output, at + m + 1)
                        chunks = [(c, base // 2 + c, P) for c in range(4)]
                        if rows > WIN_H:
                            chunks.append((4, base // 2 + 4, GRID_W))
                        chunks += [(5, TILES, P), (6, TILES + 1, P)]
                        for c, tile, n_keys in chunks:
                            mm = pe.matmul(ps_o[m % 2][:, 0:DH], probsT[0:n_keys, m % 2, c, :],
                                           v_sb[0:n_keys, par, tile, :], start=(c == 0), stop=(c == 6))
                        mm.then_inc(summed, 1)

def pipeline(eng, count, depth, step, behind_first=None):
    for n in range(depth):
        step(n, n % 2, lambda l, n=n: 0 <= n - l < count)
        if n == 0 and behind_first is not None:
            behind_first()
    with eng.Fori(0, (count - depth) // 2) as i:
        for p in range(2):
            step(i * 2 + depth + p, (depth + p) % 2, lambda l: True)
    for n in range(count, count + depth):
        step(n, n % 2, lambda l, n=n: 0 <= n - l < count)


def mixing_phase(nc, sem, io, scratch, keep):
    LAGS = 6
    with ExitStack() as ctx:
        def sb(name, shape, dt=F32):
            return ctx.enter_context(nc.sbuf_tensor(f"mix_{name}", shape, dt))

        w_hi = sb("w_hi", [P, KD, D], F32R)
        w_lo = sb("w_lo", [P, KD, D], F32R)
        router = sb("router", [P, KD, EXPERTS])
        gate_row = sb("gate_row", [P, D])
        xin = sb("xin", [P, 2, D])
        o_b = sb("o_b", [P, 2, SG])
        o_an = sb("o_an", [P, NA])
        oT_hi = sb("oT_hi", [P, 2, KD, P], F32R)
        oT_lo = sb("oT_lo", [P, 2, KD, P], F32R)
        x_new = sb("x_new", [P, 2, D])
        x_norm = sb("x_norm", [P, 2, D])
        hT = sb("hT", [P, 2, KD, P])
        junk_o = sb("junk_o", [P, NA])
        junk_x = sb("junk_x", [P, D])
        stat = sb("stat", [P, 8, 2])
        soft = sb("soft", [P, 2, EXPERTS])
        ps_o = ctx.enter_context(nc.psum_tensor("ps_oT", [P, 2 * BANK], F32))
        ps_m = [ctx.enter_context(nc.psum_tensor(f"ps_mix{i}", [P, BANK], F32)) for i in range(2)]
        ps_x = ctx.enter_context(nc.psum_tensor("ps_xT", [P, 2 * BANK], F32))
        ps_l = ctx.enter_context(nc.psum_tensor("ps_logit", [P, BANK], F32))

        w_rounded = sem("mix_w_rounded")
        w_ok = sem("mix_w_ok")
        const_in = sem("mix_const_in")
        tile_in = [sem(f"mix_tile_in{i}") for i in range(2)]
        o_sq = sem("mix_o_sq")
        o_rstd = sem("mix_o_rstd")
        o_normed = sem("mix_o_normed")
        o_turned = sem("mix_o_turned")
        o_rounded = sem("mix_o_rounded")
        o_split = sem("mix_o_split")
        mixed = sem("mix_mixed")
        gated = sem("mix_gated")
        added = sem("mix_added")
        x_sq = sem("mix_x_sq")
        x_rstd = sem("mix_x_rstd")
        x_normed = sem("mix_x_normed")
        x_turned = sem("mix_x_turned")
        h_ok = sem("mix_h_ok")
        routed = sem("mix_routed")
        top_ok = sem("mix_top_ok")
        exped = sem("mix_exped")
        pool_link = sem("mix_pool_link")
        recip = sem("mix_recip")
        stored = [sem(f"mix_stored{i}") for i in range(2)]
        aff_ok = sem("mix_aff_ok")
        block = ctx.enter_context(nc.Block())
        w_raw = keep["w_out"]
        x_rows = io["x"][0].rearrange("(t p) n -> t p n", p=P)
        ob_rows = scratch["o_b"].rearrange("(t p) n -> t p n", p=P)
        new_rows = scratch["x_new"].rearrange("(t p) n -> t p n", p=P)
        norm_rows = scratch["x_norm"].rearrange("(t p) n -> t p n", p=P)
        out_gain = keep["small"][:, SMALL["out_norm_a"][0]:SMALL["out_norm_b"][1]]

        @block.sync
        def _(sp):
            sp.dma_start(gate_row[:, :], scratch["mod"][0:D].partition_broadcast(P)
                         ).then_inc(const_in, 16)
            sp.dma_start(router[:, :, :], io["w_router"][0].rearrange("(k p) e -> p k e", p=P)
                         ).then_inc(const_in, 16)
            with sp.Fori(0, TILES // 2) as i:
                for par in range(2):
                    sp.wait_ge(added, i * 2 + par + 1)
                    sp.dma_start(o_b[:, par], ob_rows[i * 2 + par]).then_inc(tile_in[par], 16)
                    sp.dma_start(xin[:, par], x_rows[i * 2 + par]).then_inc(tile_in[par], 16)

        @block.gpsimd
        def _(pool):
            def rstd(dst, src, n):
                pool.tensor_tensor(dst, src, keep["eps"][:, :], ALU.add).then_inc(pool_link, 1)
                pool.wait_ge(pool_link, n)
                return pool.tensor_tensor(dst, dst, keep["minus_half"][:, :], ALU.pow)

            def step(t, par, active):
                if active(0):
                    pool.wait_ge(o_sq, t + 1)
                    n = 1 if isinstance(t, int) and t == 0 else t * 2
                    rstd(stat[:, 1, par:par + 1], stat[:, 0, par:par + 1], n).then_inc(o_rstd, 1)
                if active(2):
                    pool.wait_ge(x_normed, t - 1)
                    pool.dma_start(new_rows[t - 2], x_new[:, par]).then_inc(stored[par], 16)
                    pool.dma_start(norm_rows[t - 2], x_norm[:, par]).then_inc(stored[par], 16)
                if active(1):
                    q = 1 - par
                    pool.wait_ge(x_sq, t)
                    n = t * 2 + 1 if active(0) else TILES * 2
                    rstd(stat[:, 3, q:q + 1], stat[:, 2, q:q + 1], n).then_inc(x_rstd, 1)
            pipeline(pool, TILES, LAGS, step)
            for s in stored:
                pool.wait_ge(s, 16 * TILES)

        @block.scalar
        def _(act):
            def round_w():
                for c in range(KD):
                    act.activation(w_hi[:, c, :], w_raw[:, c, :], ACT.Copy,
                                   scale=out_gain[:, c:c + 1]).then_inc(w_rounded, 1)

            def step(t, par, active):
                if active(0):
                    if not (isinstance(t, int) and t == 0):
                        act.wait_ge(o_rstd, t)
                    act.activation(junk_o[:, :], keep["o_a"][:, t, :], ACT.Square, scale=float(NA) ** -0.5,
                                   accum_out=stat[:, 0, par:par + 1]).then_inc(o_sq, 1)
                q = 1 - par
                if active(3):
                    act.wait_ge(x_turned, t - 2)
                    act.wait_ge(routed, t - 2)
                    for k in range(KD):
                        act.activation(hT[:, q, k], ps_x[:, k * P:(k + 1) * P], ACT.Identity,
                                       scale=keep["gain2"][:, k:k + 1], bias=keep["shift2"][:, k:k + 1]
                                       ).then_inc(h_ok, 1)
                if active(5):
                    act.wait_ge(top_ok, t - 4)
                    act.activation(soft[:, q], ps_l[:, 0:EXPERTS], ACT.Exp, bias=stat[:, 4, q:q + 1],
                                   accum_out=stat[:, 5, q:q + 1]).then_inc(exped, 1)
                if active(1):
                    act.wait_ge(added, t + 2)
                    if not (isinstance(t, int) and t == 1):
                        act.wait_ge(x_sq, t - 1)
                    act.activation(junk_x[:, :], x_new[:, q], ACT.Square, scale=float(D) ** -0.5,
                                   accum_out=stat[:, 2, q:q + 1]).then_inc(x_sq, 1)
            pipeline(act, TILES, LAGS, step, round_w)

        @block.vector
        def _(dve):
            dve.sem_inc(added, 2)
            dve.sem_inc(routed, 2)

            def split_w():
                for c in range(KD):
                    dve.wait_ge(w_rounded, c + 1)
                    dve.scalar_tensor_tensor(out=w_lo[:, c, :], in0=w_raw[:, c, :],
                                             scalar=out_gain[:, c:c + 1], in1=w_hi[:, c, :].bitcast(F32),
                                             op0=ALU.mult, op1=ALU.subtract).then_inc(w_ok, 1)
                dve.wait_ge(const_in, 32)

            def step(t, par, active):
                q = 1 - par

                def gate(half):
                    cols = slice(half * BANK, (half + 1) * BANK)
                    dve.wait_ge(mixed, t * 2 - 1 + half)
                    dve.tensor_tensor(x_new[:, q, cols], ps_m[half][:, :], gate_row[:, cols],
                                      ALU.mult).then_inc(gated, 1)
                if active(5):
                    dve.wait_ge(routed, t - 2)
                    dve.tensor_reduce(stat[:, 4, q:q + 1], ps_l[:, 0:EXPERTS], AX.X, ALU.max,
                                      negate=True).then_inc(top_ok, 1)
                if active(2):
                    dve.wait_ge(x_rstd, t - 1)
                    if not (isinstance(t, int) and t < 4):
                        dve.wait_ge(stored[par], (t - 2 - par) * 16)
                    dve.tensor_scalar(x_norm[:, par], x_new[:, par], stat[:, 3, par:par + 1], None,
                                      ALU.mult).then_inc(x_normed, 1)
                if active(0):
                    dve.wait_ge(o_rstd, t + 1)
                    dve.tensor_scalar(o_an[:, :], keep["o_a"][:, t, :], stat[:, 1, par:par + 1], None,
                                      ALU.mult).then_inc(o_normed, 1)
                if active(1):
                    dve.wait_ge(tile_in[q], (t - 1 - q) * 16 + 32)
                    if not (isinstance(t, int) and t < 3):
                        dve.wait_ge(stored[q], (t - 1 - q) * 16)
                    gate(0)
                if active(0):
                    dve.wait_ge(o_turned, t + 1)
                    oT = ps_o[:, :].rearrange("p (k t) -> p k t", t=P)
                    dve.tensor_copy(oT_hi[:, par], oT).then_inc(o_rounded, 1)
                    dve.wait_ge(o_rounded, t + 1)
                    dve.tensor_tensor(oT_lo[:, par], oT, oT_hi[:, par].bitcast(F32), ALU.subtract
                                      ).then_inc(o_split, 1)
                if active(6):
                    dve.wait_ge(exped, t - 5)
                    dve.reciprocal(stat[:, 6, par:par + 1], stat[:, 5, par:par + 1]).then_inc(recip, 1)
                    dve.wait_ge(recip, t - 5)
                    dve.tensor_scalar(keep["aff"][:, :, t - 6], soft[:, par], stat[:, 6, par:par + 1], None,
                                      ALU.mult).then_inc(aff_ok, 1)
                if active(1):
                    gate(1)
                    dve.wait_ge(gated, t * 2)
                    dve.tensor_tensor(x_new[:, q], x_new[:, q], xin[:, q], ALU.add).then_inc(added, 1)
            pipeline(dve, TILES, LAGS, step, split_w)

        @block.tensor
        def _(pe):
            ident = keep["ident"]

            def mix(t, q, half):
                cols = slice(half * BANK, (half + 1) * BANK)
                if not (isinstance(t, int) and t == 1):
                    pe.wait_ge(gated, t * 2 - 3 + half)
                for k in range(KD):
                    if isinstance(t, int) and t == 1:
                        pe.wait_ge(w_ok, k + 1)
                    for x, (o, w) in enumerate(((oT_hi, w_hi), (oT_lo, w_hi), (oT_hi, w_lo))):
                        mm = pe.matmul(ps_m[half][:, :], o[:, q, k, :], w[:, k, cols],
                                       start=(k == 0 and x == 0), stop=(k == KD - 1 and x == 2))
                mm.then_inc(mixed, 1)

            def step(t, par, active):
                if active(1):
                    pe.wait_ge(o_split, t)
                    mix(t, 1 - par, 0)
                if active(0):
                    pe.wait_ge(tile_in[par], (t - par) * 16 + 32)
                    pe.wait_ge(o_normed, t + 1)
                    for k in range(KD):
                        src = o_an[:, k * P:(k + 1) * P] if k < KNA else o_b[:, par, (k - KNA) * P:(k - KNA + 1) * P]
                        tr = pe.transpose(ps_o[:, k * P:(k + 1) * P], src, ident[:, :])
                    tr.then_inc(o_turned, 1)
                if active(1):
                    mix(t, 1 - par, 1)
                if active(2):
                    pe.wait_ge(x_normed, t - 1)
                    if not (isinstance(t, int) and t == 2):
                        pe.wait_ge(h_ok, (t - 2) * KD)
                    for k in range(KD):
                        tr = pe.transpose(ps_x[:, k * P:(k + 1) * P], x_norm[:, par, k * P:(k + 1) * P],
                                          ident[:, :])
                    tr.then_inc(x_turned, 1)
                if active(4):
                    pe.wait_ge(h_ok, (t - 3) * KD)
                    if not (isinstance(t, int) and t == 4):
                        pe.wait_ge(exped, t - 4)
                    for k in range(KD):
                        mm = pe.matmul(ps_l[:, 0:EXPERTS], hT[:, par, k, :], router[:, k, :],
                                       start=(k == 0), stop=(k == KD - 1))
                    mm.then_inc(routed, 1)
            pipeline(pe, TILES, LAGS, step)

BITS = 30
DIGIT = 2
ROUNDS = BITS // DIGIT
TRIALS = 2 ** DIGIT - 1
UNROLL = 5


def expert_phase(nc, sem, io, scratch, keep):
    U = 18
    PAIRS = 6
    FC = 2 * P
    RAW, SPLIT, AHEAD = 6, 3, 2
    HALVES = CAP // P
    VALS = 5
    w_gate = io["w_gate"][0].rearrange("e (k p) (u n) -> e u p k n", p=P, n=FC)
    w_up = io["w_up"][0].rearrange("e (k p) (u n) -> e u p k n", p=P, n=FC)
    w_down = io["w_down"][0].rearrange("e (u k p) n -> e u p k n", p=P, k=FC // P)
    with ExitStack() as ctx:
        def sb(name, shape, dt=F32):
            return ctx.enter_context(nc.sbuf_tensor(f"moe_{name}", shape, dt))

        raw = sb("raw", [P, RAW, KD * FC])
        w_hi = sb("w_hi", [P, SPLIT, KD * FC], F32R)
        w_lo = sb("w_lo", [P, SPLIT, KD * FC], F32R)
        xs = sb("xs", [P, HALVES, D])
        xs_full = sb("xs_full", [P, KD, CAP])
        xT_hi = sb("xT_hi", [P, KD, CAP], F32R)
        xT_lo = sb("xT_lo", [P, KD, CAP], F32R)
        silu_g = sb("silu_g", [P, 2, 2 * CAP])
        g_full = sb("g_full", [P, 2, 2 * CAP])
        g_hi = sb("g_hi", [P, PAIRS, 2 * CAP], F32R)
        g_lo = sb("g_lo", [P, PAIRS, 2 * CAP], F32R)
        y = sb("y", [P, HALVES, D])
        gate_row = sb("gate_row", [P, D])
        ones_b = sb("ones_b", [P, P], BF16)
        upto_b = sb("upto_b", [P, P], BF16)
        place = sb("place", [P, ROUNDS * TRIALS], U32)
        digit = sb("digit", [P, ROUNDS * TRIALS], U32)
        digits = sb("digits", [P, ROUNDS * TRIALS], U32)
        cut = sb("cut", [P, EXPERTS])
        trial = sb("trial", [P, TRIALS, EXPERTS])
        kept = sb("kept", [P, TRIALS, EXPERTS])
        best = sb("best", [P, EXPERTS])
        reached = sb("reached", [P, TILES, TRIALS, EXPERTS], BF16)
        need = sb("need", [P, EXPERTS])
        above_b = sb("above_b", [P, EXPERTS, TILES], BF16)
        equal_b = sb("equal_b", [P, EXPERTS, TILES], BF16)
        picked_b = sb("picked_b", [P, EXPERTS, TILES], BF16)
        slot_of = sb("slot_of", [P, EXPERTS, TILES])
        iota_i = sb("iota_i", [P, CAP], U32)
        slot_row = sb("slot_row", [P, CAP], BF16)
        vals = sb("vals", [P, EXPERTS, TILES, VALS], BF16)
        rest = sb("rest", [P, EXPERTS, TILES])
        aff_rest = sb("aff_rest", [P, EXPERTS, TILES])
        tile_i = sb("tile_i", [P, TILES], U32)
        part = sb("part", [P, 1], U32)
        one_hot = sb("one_hot", [P, TILES, CAP], BF16)
        pick = sb("pick", [P, HALVES, VALS])
        pick_sum = sb("pick_sum", [P, HALVES])
        idx_next = sb("idx_next", [P, HALVES], U32)
        idx_now = sb("idx_now", [P, HALVES], U32)
        gate_next = sb("gate_next", [P, HALVES])
        gate_now = sb("gate_now", [P, HALVES])
        bank = [ctx.enter_context(nc.psum_tensor(f"moe_bank{i}", [P, BANK], F32)) for i in range(8)]

        w_in = [sem(f"moe_w_in{i}") for i in range(RAW)]
        w_rounded = sem("moe_w_rounded")
        w_split = sem("moe_w_split")
        product = sem("moe_product")
        silu_ok = sem("moe_silu_ok")
        g_ok = sem("moe_g_ok")
        g_rounded = sem("moe_g_rounded")
        g_split = sem("moe_g_split")
        xs_in = sem("moe_xs_in")
        xs_turned = sem("moe_xs_turned")
        xs_ok = sem("moe_xs_ok")
        x_rounded = sem("moe_x_rounded")
        x_split = sem("moe_x_split")
        y_ok = sem("moe_y_ok")
        y_added = sem("moe_y_added")
        hot_ok = sem("moe_hot_ok")
        picked = sem("moe_picked")
        idx_ok = sem("moe_idx_ok")
        idx_kept = sem("moe_idx_kept")
        row_in = sem("moe_row_in")
        consts = sem("moe_consts")
        passed = sem("moe_passed")
        pool_own = sem("moe_pool_own")
        chain = sem("moe_chain")
        vals_ok = sem("moe_vals_ok")
        marked = sem("moe_marked")
        counted = sem("moe_counted")
        rank_in = sem("moe_rank_in")
        ranked = sem("moe_ranked")
        dve_own = sem("moe_dve_own")
        block = ctx.enter_context(nc.Block())

        def next_expert(e, u):
            return (e, u + AHEAD) if u + AHEAD < U else (e + 1, u + AHEAD - U)

        @block.sync
        def _(sp):
            sp.dma_start(gate_row[:, :], scratch["mod"][3 * D:4 * D].partition_broadcast(P)
                         ).then_inc(row_in, 16)

            def load(expert, n, u):
                sp.wait_ge(w_split, n * U + u + 1)
                src = w_down[expert, u - 2 * PAIRS] if u >= 2 * PAIRS else (w_gate, w_up)[u % 2][expert, u // 2]
                dst = raw[:, u % RAW].rearrange("p (k n) -> p k n", n=src.shape[-1])
                sp.dma_start(dst, src).then_inc(w_in[u % RAW], 16)
            with sp.Fori(0, EXPERTS) as e:
                for u in range(U):
                    load(e, e, u)
            for u in range(AHEAD):
                load(0, EXPERTS, u)

        @block.gpsimd
        def _(pool):
            pool.iota(place[:, :], pattern=[[-DIGIT, ROUNDS], [0, TRIALS]], base=BITS - DIGIT,
                      channel_multiplier=0).then_inc(consts, 1)
            pool.iota(digit[:, :], pattern=[[0, ROUNDS], [1, TRIALS]], base=1,
                      channel_multiplier=0).then_inc(consts, 1)
            pool.memset(ones_b[:, :], 1.0).then_inc(consts, 1)
            own = Chain(pool, pool_own)
            pool.wait_ge(consts, 3)
            own(pool.affine_select(out=upto_b[:, :], in_=ones_b[:, :], compare_op=ALU.is_ge, fill=0.0, base=0,
                                   pattern=[[1, P]], channel_multiplier=-1))
            own(pool.iota(iota_i[:, :], pattern=[[1, CAP]], base=1, channel_multiplier=0))
            own(pool.iota(tile_i[:, :], pattern=[[1, TILES]], base=0, channel_multiplier=0))
            own(pool.iota(part[:, :], pattern=[[0, 1]], base=0, channel_multiplier=1))
            own(pool.tensor_copy(slot_row[:, :], iota_i[:, :]))
            wide = [P, EXPERTS, TILES]
            aff = keep["aff"]
            own(pool.tensor_copy(vals[:, :, :, 0], part[:, :, None].broadcast_to(wide)))
            own(pool.tensor_copy(vals[:, :, :, 1], tile_i[:, None, :].broadcast_to(wide)))
            own(pool.tensor_copy(vals[:, :, :, 2], aff[:, :, :]))
            own(pool.tensor_tensor(aff_rest[:, :, :], aff[:, :, :], vals[:, :, :, 2], ALU.subtract))
            own(pool.tensor_copy(vals[:, :, :, 3], aff_rest[:, :, :]))
            pool.tensor_tensor(vals[:, :, :, 4], aff_rest[:, :, :], vals[:, :, :, 3], ALU.subtract
                               ).then_inc(vals_ok, 1)

            def gather(n, before=None):
                if before is not None:
                    pool.wait_ge(xs_turned, before + 1)
                pool.wait_ge(idx_ok, n + 1)
                apart(pool, passed)
                for m in range(HALVES):
                    pool.indirect_dma_start(
                        out=xs[:, m, :], out_offset=None, in_=scratch["x_norm"],
                        in_offset=bass.IndirectOffsetOnAxis(ap=idx_next[:, m:m + 1], axis=0)
                    ).then_inc(xs_in, 16)
            gather(0)
            with pool.Fori(0, EXPERTS) as e:
                pool.wait_ge(idx_ok, e + 1)
                apart(pool, passed)
                pool.tensor_copy(idx_now[:, :], idx_next[:, :]).then_inc(idx_kept, 1)
                gather(e + 1, e)
                pool.wait_ge(y_ok, e * 4 + 8)
                pool.wait_ge(idx_kept, e + 1)
                apart(pool, passed)
                for m in range(HALVES):
                    pool.indirect_dma_start(
                        out=scratch["x_new"],
                        out_offset=bass.IndirectOffsetOnAxis(ap=idx_now[:, m:m + 1], axis=0),
                        in_=y[:, m, :], in_offset=None, compute_op=ALU.add).then_inc(y_added, 16)
                pool.wait_ge(y_added, (e + 1) * 16 * HALVES)
            pool.wait_ge(xs_in, (EXPERTS + 1) * 16 * HALVES)

        @block.scalar
        def _(act):
            def split(n, u):
                act.wait_ge(w_in[u % RAW], (n * (U // RAW) + u // RAW + 1) * 16)
                act.wait_ge(product, n * U + u + 1)
                act.activation(w_hi[:, u % SPLIT], raw[:, u % RAW], ACT.Copy).then_inc(w_rounded, 1)

            def modulate(n):
                act.wait_ge(xs_turned, n + 1)
                for k in range(KD):
                    act.activation(xs_full[:, k], bank[k // 2][:, (k % 2) * CAP:(k % 2 + 1) * CAP],
                                   ACT.Identity, scale=keep["gain2"][:, k:k + 1],
                                   bias=keep["shift2"][:, k:k + 1]).then_inc(xs_ok, 1)
            for u in range(AHEAD):
                split(0, u)
            modulate(0)
            with act.Fori(0, EXPERTS) as e:
                for u in range(U):
                    split(*next_expert(e, u))
                    if u % 2 and u < 2 * PAIRS:
                        i = u // 2
                        act.wait_ge(product, e * U + u + 3)
                        act.wait_ge(g_ok, e * PAIRS + i + 1)
                        act.activation(silu_g[:, i % 2], bank[i % 2][:, :], ACT.Silu).then_inc(silu_ok, 1)
                    if u % 2 == 0 and 2 <= u <= 2 * PAIRS:
                        i = u // 2 - 1
                        act.wait_ge(g_ok, e * PAIRS + i + 3)
                        act.activation(g_hi[:, i], g_full[:, i % 2], ACT.Copy).then_inc(g_rounded, 1)
                    if u == 14:
                        modulate(e + 1)

        @block.vector
        def _(dve):
            for s, v in ((w_split, RAW), (product, SPLIT), (silu_ok, 2), (g_ok, 2), (y_ok, 4)):
                dve.sem_inc(s, v)
            own = Chain(dve, chain)

            def split(n, u):
                dve.wait_ge(w_rounded, n * U + u + 1)
                dve.tensor_tensor(w_lo[:, u % SPLIT], raw[:, u % RAW], w_hi[:, u % SPLIT].bitcast(F32),
                                  ALU.subtract).then_inc(w_split, 1)

            aff = keep["aff"]
            dve.wait_ge(consts, 2)
            own(dve.tensor_tensor(digits[:, :], digit[:, :], place[:, :], ALU.logical_shift_left))
            own(dve.memset(cut[:, :], 0.0))
            before = own.n
            tries = [P, TILES // 2, TRIALS, EXPERTS]
            by_tile = aff[:, :, :].rearrange("p e t -> p t e")[:, :, None, :]
            with dve.Fori(0, ROUNDS // UNROLL) as i:
                for r in (i * UNROLL + n for n in range(UNROLL)):
                    step = Chain(dve, chain, before + r * 4)
                    digit_of = digits[:, bass.ds(r * TRIALS, TRIALS)]
                    step(dve.tensor_tensor(trial[:, :, :].bitcast(U32),
                                           cut[:, None, :].bitcast(U32).broadcast_to([P, TRIALS, EXPERTS]),
                                           digit_of[:, :, None].broadcast_to([P, TRIALS, EXPERTS]), ALU.bitwise_or))
                    for half in range(2):
                        ts = slice(half * TILES // 2, (half + 1) * TILES // 2)
                        dve.tensor_tensor(reached[:, ts, :, :], by_tile[:, ts].broadcast_to(tries),
                                          trial[:, None, :, :].broadcast_to(tries), ALU.is_ge).then_inc(marked, 1)
                    dve.wait_ge(counted, r + 1)
                    step(dve.scalar_tensor_tensor(
                        out=kept[:, :, :], in0=bank[0][:, 0:TRIALS * EXPERTS].rearrange("p (j e) -> p j e", j=TRIALS),
                        scalar=CAP - 0.5, in1=trial[:, :, :], op0=ALU.is_ge, op1=ALU.mult))
                    step(dve.tensor_reduce(best[:, :], kept[:, :, :].rearrange("p j e -> p e j"), AX.X, ALU.max))
                    step(dve.tensor_tensor(cut[:, :], cut[:, :], best[:, :], ALU.max))
            own = Chain(dve, chain, before + ROUNDS * 4)
            wide = cut[:, :, None].broadcast_to([P, EXPERTS, TILES])
            dve.tensor_tensor(above_b[:, :, :], aff[:, :, :], wide, ALU.is_gt).then_inc(marked, 1)
            dve.tensor_tensor(equal_b[:, :, :], aff[:, :, :], wide, ALU.is_equal).then_inc(rank_in, 1)
            dve.wait_ge(counted, ROUNDS + 1)
            own(dve.tensor_scalar(need[:, :], bank[0][:, 0:EXPERTS], -1.0, float(CAP), ALU.mult, ALU.add))
            dve.wait_ge(ranked, 1)
            own(dve.tensor_tensor(rest[:, :, :], bank[1][:, 0:EXPERTS * TILES].rearrange("p (e t) -> p e t", t=TILES),
                                  need[:, :, None].broadcast_to([P, EXPERTS, TILES]), ALU.is_le))
            own(dve.tensor_tensor(rest[:, :, :], rest[:, :, :], equal_b[:, :, :], ALU.mult))
            dve.tensor_tensor(picked_b[:, :, :], rest[:, :, :], above_b[:, :, :], ALU.add).then_inc(rank_in, 1)
            dve.wait_ge(ranked, 2)
            own(dve.tensor_tensor(slot_of[:, :, :],
                                  bank[1][:, 0:EXPERTS * TILES].rearrange("p (e t) -> p e t", t=TILES),
                                  picked_b[:, :, :], ALU.mult))
            dve.wait_ge(vals_ok, 1)

            def hot(expert, t):
                dve.tensor_scalar(one_hot[:, t], slot_row[:, :],
                                  slot_of[:, expert, t:t + 1] if isinstance(expert, int)
                                  else slot_of[:, bass.ds(expert, 1), t], None, ALU.is_equal
                                  ).then_inc(hot_ok, 1)

            def take(n, link):
                dve.wait_ge(picked, n + 1)
                link(dve.tensor_copy(pick[:, :, :], bank[4][:, 0:HALVES * 8].rearrange(
                    "p (m v) -> p m v", v=8)[:, :, 0:VALS]))
                dve.scalar_tensor_tensor(out=idx_next[:, :], in0=pick[:, :, 1], scalar=float(P),
                                         in1=pick[:, :, 0], op0=ALU.mult, op1=ALU.add).then_inc(idx_ok, 1)
                link(dve.tensor_tensor(pick_sum[:, :], pick[:, :, 2], pick[:, :, 3], ALU.add))
                link(dve.tensor_tensor(gate_next[:, :], pick_sum[:, :], pick[:, :, 4], ALU.add))

            def split_tokens(n):
                for half in range(2):
                    ks = slice(half * KD // 2, (half + 1) * KD // 2)
                    dve.wait_ge(xs_ok, n * KD + (half + 1) * KD // 2)
                    dve.tensor_copy(xT_hi[:, ks, :], xs_full[:, ks, :]).then_inc(x_rounded, 1)
                    dve.wait_ge(x_rounded, n * 2 + half + 1)
                    dve.tensor_tensor(xT_lo[:, ks, :], xs_full[:, ks, :], xT_hi[:, ks, :].bitcast(F32),
                                      ALU.subtract).then_inc(x_split, 1)
            for t in range(TILES):
                hot(0, t)
            take(0, own)
            for u in range(AHEAD):
                split(0, u)
            split_tokens(0)
            dve.wait_ge(row_in, 16)
            LINKS = 4
            with dve.Fori(0, EXPERTS) as e:
                link = Chain(dve, dve_own, e * LINKS)
                for u in range(U):
                    split(*next_expert(e, u))
                    if u == 0:
                        dve.wait_ge(y_ok, e * 4 + 4)
                        link(dve.tensor_copy(gate_now[:, :], gate_next[:, :]))
                    if u < 4:
                        if u == 0:
                            dve.wait_ge(picked, e + 1)
                        for t in range(4 * u, 4 * u + 4):
                            hot((e + 1) % EXPERTS, t)
                    if u == 8:
                        dve.wait_ge(idx_kept, e + 1)
                        take(e + 1, link)
                    if u % 2 == 0 and 2 <= u <= 2 * PAIRS:
                        i = u // 2 - 1
                        dve.wait_ge(product, e * U + u + 3)
                        dve.wait_ge(silu_ok, e * PAIRS + i + 3)
                        dve.tensor_tensor(g_full[:, i % 2], bank[2 + i % 2][:, :], silu_g[:, i % 2], ALU.mult
                                          ).then_inc(g_ok, 1)
                    if u % 2 and 3 <= u <= 2 * PAIRS + 1:
                        i = (u - 3) // 2
                        dve.wait_ge(g_rounded, e * PAIRS + i + 1)
                        dve.tensor_tensor(g_lo[:, i], g_full[:, i % 2], g_hi[:, i].bitcast(F32), ALU.subtract
                                          ).then_inc(g_split, 1)
                    if u == 15:
                        split_tokens(e + 1)
                dve.wait_ge(product, e * U + U + 3)
                for m in range(HALVES):
                    for half in range(2):
                        cols = slice(half * BANK, (half + 1) * BANK)
                        dve.scalar_tensor_tensor(out=y[:, m, cols], in0=bank[4 + 2 * m + half][:, :],
                                                 scalar=gate_now[:, m:m + 1], in1=gate_row[:, cols],
                                                 op0=ALU.mult, op1=ALU.mult).then_inc(y_ok, 1)
                assert link.n == LINKS

        @block.tensor
        def _(pe):
            ident = keep["ident"]
            pe.wait_ge(consts, 3)
            pe.wait_ge(pool_own, 1)
            with pe.Fori(0, ROUNDS // UNROLL) as i:
                for r in (i * UNROLL + n for n in range(UNROLL)):
                    for t in range(TILES):
                        if t % (TILES // 2) == 0:
                            pe.wait_ge(marked, r * 2 + 1 + t // (TILES // 2))
                        mm = pe.matmul(bank[0][:, 0:TRIALS * EXPERTS], ones_b[:, :],
                                       reached[:, t, :, :].rearrange("p j e -> p (j e)"),
                                       start=(t == 0), stop=(t == TILES - 1))
                    mm.then_inc(counted, 1)
            pe.wait_ge(marked, ROUNDS * 2 + 1)
            for t in range(TILES):
                mm = pe.matmul(bank[0][:, 0:EXPERTS], ones_b[:, :], above_b[:, :, t],
                               start=(t == 0), stop=(t == TILES - 1))
            mm.then_inc(counted, 1)
            for r, marks in enumerate((equal_b, picked_b)):
                pe.wait_ge(rank_in, r + 1)
                rank = bank[1][:, 0:EXPERTS * TILES].rearrange("p (e t) -> p e t", t=TILES)
                for d in range(TILES - 1, 0, -1):
                    pe.matmul(rank[:, :, d:], ones_b[:, :], marks[:, :, 0:TILES - d],
                              start=(d == TILES - 1), stop=False, skip_group_check=True)
                mm = pe.matmul(rank, upto_b[:, :], marks[:, :, :], start=False, stop=True,
                               skip_group_check=True)
                mm.then_inc(ranked, 1)

            def take(expert, n):
                pe.wait_ge(hot_ok, (n + 1) * TILES)
                for m in range(HALVES):
                    for t in range(TILES):
                        row = (vals[:, expert, t, :] if isinstance(expert, int)
                               else vals[:, bass.ds(expert, 1), t, :].rearrange("p a v -> p (a v)"))
                        mm = pe.matmul(bank[4][:, m * 8:m * 8 + VALS], one_hot[:, t, m * P:(m + 1) * P], row,
                                       start=(t == 0), stop=(t == TILES - 1))
                mm.then_inc(picked, 1)

            def turn(n):
                pe.wait_ge(xs_in, (n + 1) * 16 * HALVES)
                for k in range(KD):
                    for m in range(HALVES):
                        a = (k % 2) * CAP + m * P
                        tr = pe.transpose(bank[k // 2][:, a:a + P], xs[:, m, k * P:(k + 1) * P], ident[:, :])
                tr.then_inc(xs_turned, 1)
            take(0, 0)
            turn(0)
            with pe.Fori(0, EXPERTS) as e:
                for u in range(U):
                    if u == 7:
                        pe.wait_ge(y_ok, e * 4 + 4)
                        take((e + 1) % EXPERTS, e + 1)
                    if u == 13:
                        pe.wait_ge(g_ok, (e + 1) * PAIRS + 2)
                        turn(e + 1)
                    pe.wait_ge(w_split, e * U + u + 1 + RAW)
                    wh, wl = w_hi[:, u % SPLIT], w_lo[:, u % SPLIT]
                    if u < 2 * PAIRS:
                        i = u // 2
                        pe.wait_ge(g_ok if u % 2 else silu_ok, e * PAIRS + i + 1)
                        b = bank[i % 2 + 2 * (u % 2)]
                        for j in range(2):
                            for k in range(KD):
                                if u == 0 and j == 0 and k % (KD // 2) == 0:
                                    pe.wait_ge(x_split, e * 2 + 1 + k // (KD // 2))
                                cols = slice(k * FC + j * P, k * FC + (j + 1) * P)
                                for x, (w, h) in enumerate(((wh, xT_hi), (wh, xT_lo), (wl, xT_hi))):
                                    mm = pe.matmul(b[:, j * CAP:(j + 1) * CAP], w[:, cols], h[:, k, :],
                                                   start=(k == 0 and x == 0), stop=(k == KD - 1 and x == 2))
                    else:
                        i = u - 2 * PAIRS
                        if i == 0:
                            pe.wait_ge(idx_ok, e + 2)
                        pe.wait_ge(g_split, e * PAIRS + i + 1)
                        for j in range(2):
                            for m in range(HALVES):
                                toks = slice(j * CAP + m * P, j * CAP + (m + 1) * P)
                                for half in range(2):
                                    cols = slice(j * D + half * BANK, j * D + (half + 1) * BANK)
                                    for x, (g, w) in enumerate(((g_hi, wh), (g_lo, wh), (g_hi, wl))):
                                        mm = pe.matmul(bank[4 + 2 * m + half][:, :], g[:, i, toks], w[:, cols],
                                                       start=(i == 0 and j == 0 and x == 0),
                                                       stop=(i == PAIRS - 1 and j == 1 and x == 2))
                    mm.then_inc(product, 1)


def final_phase(nc, sem, io, scratch, keep, out):
    with ExitStack() as ctx:
        def sb(name, shape, dt=F32):
            return ctx.enter_context(nc.sbuf_tensor(f"fin_{name}", shape, dt))

        RING = 8
        x = sb("x", [P, RING, D])
        junk = sb("junk", [P, RING, D])
        gain = sb("gain", [P, D])
        stat = sb("stat", [P, RING, 2])
        gain_in = sem("fin_gain_in")
        x_in = [sem(f"fin_x_in{i}") for i in range(RING)]
        squared = sem("fin_squared")
        pool_own = sem("fin_pool_own")
        rooted = sem("fin_rooted")
        scaled = sem("fin_scaled")
        stored = [sem(f"fin_stored{i}") for i in range(RING)]
        block = ctx.enter_context(nc.Block())
        x_rows = scratch["x_new"].rearrange("(i t p) n -> i t p n", p=P, t=RING)
        out_rows = out[0].rearrange("(i t p) n -> i t p n", p=P, t=RING)
        STEPS = TILES // RING

        @block.sync
        def _(sp):
            sp.dma_start(gain[:, :], io["norm_final"].partition_broadcast(P)).then_inc(gain_in, 16)
            with sp.Fori(0, STEPS) as i:
                for t in range(RING):
                    sp.wait_ge(stored[t], (i + 1) * 16)
                    sp.dma_start(x[:, t], x_rows[i, t]).then_inc(x_in[t], 16)

        @block.scalar
        def _(act):
            for s in stored:
                act.sem_inc(s, 16)

            def store(i, t):
                act.wait_ge(scaled, i * RING + t + 1)
                act.dma_start(out_rows[i, t], x[:, t]).then_inc(stored[t], 16)
            with act.Fori(0, STEPS) as i:
                for t in range(RING):
                    act.wait_ge(x_in[t], (i + 1) * 16)
                    act.activation(junk[:, t], x[:, t], ACT.Square, scale=float(D) ** -0.5,
                                   accum_out=stat[:, t, 0:1]).then_inc(squared, 1)
                    if t >= 2:
                        store(i, t - 2)
                store(i, RING - 2)
                store(i, RING - 1)
            for s in stored:
                act.wait_ge(s, 16 * (STEPS + 1))

        @block.gpsimd
        def _(pool):
            with pool.Fori(0, STEPS) as i:
                for t in range(RING):
                    pool.wait_ge(squared, i * RING + t + 1)
                    pool.tensor_tensor(stat[:, t, 1:2], stat[:, t, 0:1], keep["eps"][:, :], ALU.add
                                       ).then_inc(pool_own, 1)
                    pool.wait_ge(pool_own, i * RING + t + 1)
                    pool.tensor_tensor(stat[:, t, 1:2], stat[:, t, 1:2], keep["minus_half"][:, :], ALU.pow
                                       ).then_inc(rooted, 1)

        @block.vector
        def _(dve):
            dve.wait_ge(gain_in, 16)
            with dve.Fori(0, STEPS) as i:
                for t in range(RING):
                    dve.wait_ge(rooted, i * RING + t + 1)
                    dve.scalar_tensor_tensor(out=x[:, t], in0=x[:, t], scalar=stat[:, t, 1:2], in1=gain[:, :],
                                             op0=ALU.mult, op1=ALU.mult).then_inc(scaled, 1)

def hybrid_layer_kernel(nc, io, out):
    with ExitStack() as ctx:
        taken = []

        def sem(name):
            taken.append(nc.alloc_semaphore(name))
            return taken[-1]

        def phase(build, *args):
            build(nc, sem, *args)
            nc.clear_and_free_semaphores(taken)
            nc.all_engine_barrier()
            taken.clear()

        def sb(name, shape):
            return ctx.enter_context(nc.sbuf_tensor(name, shape, F32))

        def dram(name, shape):
            return nc.dram_tensor(name, shape, F32, kind="Internal").ap()

        scratch = {
            "mod": dram("mod_dram", ((N_MOD - EARLY) * D,)),
            "rel": dram("rel_dram", (HEADS * RPB_H, GRID_W, 2 * GRID_W)),
            "table": dram("table_dram", (P, HEADS, SLOTS, GRID_W)),
            "qT": dram("qT_dram", (NA, SEQ)),
            "kT": dram("kT_dram", (NA, SEQ)),
            "v": dram("v_dram", (SEQ, NA)),
            "kTc": dram("kTc_dram", (NA, CTX)),
            "vc": dram("vc_dram", (CTX, NA)),
            "o_b": dram("o_b_dram", (SEQ, SG)),
            "x_new": dram("x_new_dram", (SEQ, D)),
            "x_norm": dram("x_norm_dram", (SEQ, D)),
        }
        keep = {"ident": sb("ident", [P, P]), "small": sb("small", [P, SMALL_ROWS]),
                "minus_half": sb("minus_half", [P, 1]), "eps": sb("eps", [P, 1]),
                "aff": sb("aff", [P, EXPERTS, TILES])}
        for name in "1c2":
            keep["gain" + name] = sb("gain" + name, [P, KD])
            keep["shift" + name] = sb("shift" + name, [P, KD])
        keep["cond"] = sb("cond", [P, 2, KD])

        def columns(a, steps):
            return a.rearrange("(a p) (s n) -> s a p n", p=P, s=steps)

        def rows(a, steps):
            return a.rearrange("(s a p) n -> s a p n", p=P, s=steps)

        phase(modulation_phase, io, scratch, keep)
        phase(projection_phase, io, scratch, keep, "ctx", rows(io["ctx"][0], 1), 1, CTX // P, "kv",
              keep["gainc"], keep["shiftc"],
              {"k": columns(scratch["kTc"], 1), "v": rows(scratch["vc"], 1)})
        phase(projection_phase, io, scratch, keep, "tok", rows(io["x"][0], 4), 4, TILES // 4, "qkvzu",
              keep["gain1"], keep["shift1"],
              {"q": columns(scratch["qT"], 4), "k": columns(scratch["kT"], 4),
               "v": rows(scratch["v"], 4), "u": rows(scratch["o_b"], 4)})
        with nc.sbuf_tensor("o_a", [P, TILES, NA], F32) as o_a, nc.sbuf_tensor("w_out", [P, KD, D], F32) as w_out:
            keep["o_a"], keep["w_out"] = o_a, w_out
            phase(attention_phase, io, scratch, keep)
            phase(mixing_phase, io, scratch, keep)
        phase(expert_phase, io, scratch, keep)
        final_phase(nc, sem, io, scratch, keep, out)


_INS = ["x", "c", "ctx", "c_ctx", "w_mod", "b_mod", "norm1", "w_in", "rpb", "w_s", "b_s", "gmlp_norm",
        "out_norm_a", "out_norm_b", "w_out", "norm2", "w_router", "w_gate", "w_up", "w_down", "norm_final"]
_OUTS = [((1, SEQ, D), "float32")]


def kernel(**inputs):
    import numpy as _np
    import concourse.bacc as _bacc
    from concourse import mybir as _mybir
    from concourse.bass_utils import run_bass_kernel_spmd as _run

    nc = _bacc.Bacc("TRN2", target_bir_lowering=False, num_devices=1)
    arrays, io = {}, {}
    for name in _INS:
        a = _np.ascontiguousarray(inputs[name])
        arrays[f"in_{name}_dram"] = a
        io[name] = nc.dram_tensor(f"in_{name}_dram", a.shape, _mybir.dt.from_np(a.dtype), kind="ExternalInput").ap()
    outs = []
    for i, (shape, dtype) in enumerate(_OUTS):
        dt = _mybir.dt.from_np(_np.dtype(dtype))
        outs.append(nc.dram_tensor(f"out_{i}_dram", shape, dt, kind="ExternalOutput").ap())
    hybrid_layer_kernel(nc, io, outs[0])
    r = _run(nc, [arrays], core_ids=[0])
    got = tuple(r.results[0][f"out_{i}_dram"] for i in range(len(_OUTS)))
    return got[0]
```
